# Optimizing a Trainium2 kernel written in Bass

```python
import math
import jax, jax.numpy as jnp
from jax import lax
import numpy as np

D_MODEL = 1024
BATCH = 1
SEQ = 256
DEPTH = 2

MIX_WIDTH = D_MODEL
GDN_HEADS = 4
GDN_HEAD_DIM = 128
GDN_WIDTH = GDN_HEADS * GDN_HEAD_DIM
GDN_CONV = 4
GDN_CHUNK = 64
NSA_HEADS = 8
NSA_KV_HEADS = 2
NSA_HEAD_DIM = 64
NSA_WIDTH = NSA_HEADS * NSA_HEAD_DIM
NSA_KV_WIDTH = NSA_KV_HEADS * NSA_HEAD_DIM
CMP_LEN = 32
CMP_STRIDE = 16
CMP_HIDDEN = 2 * NSA_HEAD_DIM
SEL_BLOCK = 64
N_SELECT = 16
WINDOW = 512
Q_BLOCK = 128
ROPE_THETA = 500000.0
ROT_DIM = NSA_HEAD_DIM // 4
D_FF = 2816
N_ADA = 9
NORM_EPS = 1e-6
IN_SIZES = (3 * GDN_WIDTH, GDN_WIDTH, GDN_HEADS, GDN_HEADS,
            NSA_WIDTH, NSA_KV_WIDTH, NSA_KV_WIDTH, NSA_KV_WIDTH,
            NSA_KV_WIDTH, NSA_KV_WIDTH, NSA_KV_WIDTH, 3 * NSA_HEADS)
IN_WIDTH = sum(IN_SIZES)


def rms_norm(x, g):
    xf = x.astype(jnp.float32)
    y = xf * lax.rsqrt(jnp.mean(xf * xf, axis=-1, keepdims=True) + NORM_EPS)
    return (y * g.astype(jnp.float32)).astype(x.dtype)

def l2_norm(x):
    xf = x.astype(jnp.float32)
    return xf * lax.rsqrt(jnp.sum(xf * xf, axis=-1, keepdims=True) + NORM_EPS)

def modulate(h, shift, scale):
    return h * (1.0 + scale[:, None, :]) + shift[:, None, :]

def swiglu(h, w_in, w_out):
    gate, up = jnp.split(h @ w_in, 2, axis=-1)
    return (jax.nn.silu(gate) * up) @ w_out

def split_cols(x, sizes):
    offs = [int(o) for o in np.cumsum(sizes)[:-1]]
    return jnp.split(x, offs, axis=-1)

def masked_softmax(s, mask):
    s = jnp.where(mask, s.astype(jnp.float32), -jnp.inf)
    m = jnp.max(s, axis=-1, keepdims=True)
    m = jnp.where(jnp.isfinite(m), m, 0.0)
    p = jnp.exp(s - m)
    return p / jnp.maximum(jnp.sum(p, axis=-1, keepdims=True), 1e-30)

def partial_rope(x, cos, sin):
    half = ROT_DIM // 2
    xf = x[..., :ROT_DIM].astype(jnp.float32)
    x1, x2 = xf[..., :half], xf[..., half:]
    rot = jnp.concatenate([x1 * cos - x2 * sin, x2 * cos + x1 * sin], axis=-1).astype(x.dtype)
    return jnp.concatenate([rot, x[..., ROT_DIM:]], axis=-1)

def causal_dwconv(x, w):
    k = w.shape[0]
    return lax.conv_general_dilated(
        x, w[:, None, :].astype(x.dtype), window_strides=(1,), padding=[(k - 1, 0)],
        dimension_numbers=("NWC", "WIO", "NWC"), feature_group_count=x.shape[-1])

def chunk_gated_delta_rule(q, k, v, g, beta):
    B, T, H, Dk = q.shape
    Dv = v.shape[-1]
    C = GDN_CHUNK
    N = T // C

    def chunks(t):
        t = t.astype(jnp.float32).reshape((B, N, C, H) + t.shape[3:])
        return jnp.moveaxis(t, (1, 3), (0, 2))

    qc, kc, vc, bc = chunks(q), chunks(k), chunks(v), chunks(beta)
    gc = jnp.cumsum(chunks(g), axis=-1)
    causal = jnp.tril(jnp.ones((C, C), dtype=bool))
    strict = jnp.tril(jnp.ones((C, C), dtype=bool), -1)
    decay = jnp.exp(jnp.where(causal, gc[..., :, None] - gc[..., None, :], -jnp.inf))
    kb = kc * bc[..., None]
    lower = jnp.where(strict, jnp.einsum("nbhcd,nbhsd->nbhcs", kb, kc) * decay, 0.0)
    rhs = jnp.concatenate([vc * bc[..., None], kb * jnp.exp(gc)[..., None]], axis=-1)
    sol = lax.linalg.triangular_solve(lower, rhs, left_side=True, lower=True, unit_diagonal=True)
    u, w = sol[..., :Dv], sol[..., Dv:]

    def step(S, xs):
        q_i, k_i, u_i, w_i, g_i, d_i = xs
        v_new = u_i - jnp.einsum("bhcd,bhdv->bhcv", w_i, S)
        attn = jnp.einsum("bhcd,bhsd->bhcs", q_i, k_i) * d_i
        o = (jnp.einsum("bhcd,bhdv->bhcv", q_i * jnp.exp(g_i)[..., None], S)
             + jnp.einsum("bhcs,bhsv->bhcv", attn, v_new))
        g_last = g_i[..., -1:]
        S = (S * jnp.exp(g_last)[..., None]
             + jnp.einsum("bhcd,bhcv->bhdv", k_i * jnp.exp(g_last - g_i)[..., None], v_new))
        return S, o

    S0 = jnp.zeros((B, H, Dk, Dv), jnp.float32)
    _, o = lax.scan(step, S0, (qc, kc, u, w, gc, decay))
    return jnp.moveaxis(o, (0, 2), (1, 3)).reshape(B, T, H, Dv)

def gated_deltanet(qkv, z, b_raw, a_raw, conv_w, a_log, dt_bias, norm_g):
    B, T, _ = qkv.shape
    qkv = jax.nn.silu(causal_dwconv(qkv, conv_w))
    q, k, v = jnp.split(qkv, 3, axis=-1)
    hd = (B, T, GDN_HEADS, GDN_HEAD_DIM)
    q = l2_norm(q.reshape(hd)) * (GDN_HEAD_DIM ** -0.5)
    k = l2_norm(k.reshape(hd))
    v = v.reshape(hd)
    beta = jax.nn.sigmoid(b_raw.astype(jnp.float32))
    g = -jnp.exp(a_log.astype(jnp.float32)) * jax.nn.softplus(a_raw.astype(jnp.float32) + dt_bias.astype(jnp.float32))
    o = chunk_gated_delta_rule(q, k, v, g, beta)
    o = rms_norm(o, norm_g) * jax.nn.silu(z.reshape(hd).astype(jnp.float32))
    return o.reshape(B, T, GDN_WIDTH).astype(qkv.dtype)

def native_sparse_attention(q, kc, vc, ks, vs, kw, vw, gate_raw, cos, sin,
                            pe_k, w1_k, w2_k, pe_v, w1_v, w2_v, out_norm_g):
    B, T, _ = q.shape
    Hq, G, dh = NSA_HEADS, NSA_KV_HEADS, NSA_HEAD_DIM
    R = Hq // G
    scale = dh ** -0.5
    q = partial_rope(q.reshape(B, T, Hq, dh), cos, sin).reshape(B, T, G, R, dh)
    heads = lambda t: t.reshape(B, T, G, dh)
    kc = partial_rope(heads(kc), cos, sin)
    ks = partial_rope(heads(ks), cos, sin)
    kw = partial_rope(heads(kw), cos, sin)
    vc, vs, vw = heads(vc), heads(vs), heads(vw)

    n_cmp = (T - CMP_LEN) // CMP_STRIDE + 1
    cmp_idx = np.arange(n_cmp)[:, None] * CMP_STRIDE + np.arange(CMP_LEN)[None, :]

    def compress(t, pe, w1, w2):
        blk = t[:, cmp_idx] + pe[:, None, :]
        blk = jnp.moveaxis(blk, 3, 2).reshape(B, n_cmp, G, CMP_LEN * dh)
        return jax.nn.silu(blk @ w1) @ w2

    k_cmp = compress(kc, pe_k, w1_k, w2_k)
    v_cmp = compress(vc, pe_v, w1_v, w2_v)
    cmp_end = jnp.asarray(cmp_idx[:, -1])

    n_blk = T // SEL_BLOCK
    n_sel = min(N_SELECT, n_blk)
    sel_start = np.arange(n_blk) * SEL_BLOCK
    overlap = jnp.asarray(((cmp_idx[:, :1] < sel_start[None, :] + SEL_BLOCK)
                           & (cmp_idx[:, -1:] >= sel_start[None, :])).astype(np.float32))
    blk_ids = jnp.arange(n_blk)
    ks_t = jnp.moveaxis(ks, 2, 1)
    vs_t = jnp.moveaxis(vs, 2, 1)
    b_ix = jnp.arange(B)[:, None, None, None]
    g_ix = jnp.arange(G)[None, :, None, None]
    kw_pad = jnp.pad(kw, ((0, 0), (WINDOW, 0), (0, 0), (0, 0)))
    vw_pad = jnp.pad(vw, ((0, 0), (WINDOW, 0), (0, 0), (0, 0)))
    gates = jax.nn.sigmoid(gate_raw.astype(jnp.float32)).reshape(B, T, G, R, 3)

    def one_block(i):
        s = i * Q_BLOCK
        t = s + jnp.arange(Q_BLOCK)
        qb = lax.dynamic_slice_in_dim(q, s, Q_BLOCK, axis=1)
        gb = lax.dynamic_slice_in_dim(gates, s, Q_BLOCK, axis=1)
        sc = jnp.einsum("bqgrd,bngd->bgrqn", qb, k_cmp) * scale
        p_cmp = masked_softmax(sc, cmp_end[None, :] <= t[:, None])
        o_cmp = jnp.einsum("bgrqn,bngd->bqgrd", p_cmp.astype(v_cmp.dtype), v_cmp)
        imp = jnp.einsum("bgrqn,nj->bgqj", p_cmp, overlap)
        cur = t[:, None] // SEL_BLOCK
        forced = (blk_ids == 0) | (blk_ids == cur) | (blk_ids == cur - 1)
        valid = blk_ids * SEL_BLOCK <= t[:, None]
        imp = jnp.where(forced, jnp.inf, jnp.where(valid, imp, -jnp.inf))
        _, top = lax.top_k(imp, n_sel)
        tok = (top[..., None] * SEL_BLOCK + jnp.arange(SEL_BLOCK)).reshape(B, G, Q_BLOCK, n_sel * SEL_BLOCK)
        k_sel = ks_t[b_ix, g_ix, tok]
        v_sel = vs_t[b_ix, g_ix, tok]
        ss = jnp.einsum("bqgrd,bgqld->bgrql", qb, k_sel) * scale
        p_sel = masked_softmax(ss, (tok <= t[:, None])[:, :, None])
        o_sel = jnp.einsum("bgrql,bgqld->bqgrd", p_sel.astype(v_sel.dtype), v_sel)
        k_win = lax.dynamic_slice_in_dim(kw_pad, s, WINDOW + Q_BLOCK, axis=1)
        v_win = lax.dynamic_slice_in_dim(vw_pad, s, WINDOW + Q_BLOCK, axis=1)
        kp = s - WINDOW + jnp.arange(WINDOW + Q_BLOCK)
        win_mask = (kp[None, :] <= t[:, None]) & (kp[None, :] > t[:, None] - WINDOW) & (kp[None, :] >= 0)
        sw = jnp.einsum("bqgrd,bkgd->bgrqk", qb, k_win) * scale
        p_win = masked_softmax(sw, win_mask)
        o_win = jnp.einsum("bgrqk,bkgd->bqgrd", p_win.astype(v_win.dtype), v_win)
        o = gb[..., 0:1] * o_cmp + gb[..., 1:2] * o_sel + gb[..., 2:3] * o_win
        o = rms_norm(o, out_norm_g)
        return o.reshape(B, Q_BLOCK, NSA_WIDTH)

    out = lax.map(one_block, jnp.arange(T // Q_BLOCK))
    return jnp.moveaxis(out, 0, 1).reshape(B, T, NSA_WIDTH).astype(q.dtype)

def token_mix(h, w_in, conv_w, a_log, dt_bias, gdn_norm_g, pe_k, w1_k, w2_k,
              pe_v, w1_v, w2_v, nsa_norm_g, w_out, cos, sin):
    (qkv, z, b_raw, a_raw, q_n, kc, vc, ks, vs, kw, vw, g_raw) = split_cols(h @ w_in, IN_SIZES)
    y_gdn = gated_deltanet(qkv, z, b_raw, a_raw, conv_w, a_log, dt_bias, gdn_norm_g)
    y_nsa = native_sparse_attention(q_n, kc, vc, ks, vs, kw, vw, g_raw, cos, sin,
                                    pe_k, w1_k, w2_k, pe_v, w1_v, w2_v, nsa_norm_g)
    return jnp.concatenate([y_gdn, y_nsa.astype(y_gdn.dtype)], axis=-1) @ w_out

def first_inputs(seed: int = 0) -> dict:
    key = jax.random.key(seed)
    ks = jax.random.split(key, 24)
    nrm = lambda k, shape, s: jax.random.normal(k, shape, jnp.float32) * s
    x = nrm(ks[0], (BATCH, SEQ, D_MODEL), 1.0)
    c = nrm(ks[1], (BATCH, D_MODEL), 1.0)
    positions = (jax.random.randint(ks[2], (BATCH, 1), 0, SEQ, dtype=jnp.int32)
                 + jnp.arange(SEQ, dtype=jnp.int32)[None, :])
    ada_w = nrm(ks[3], (DEPTH, D_MODEL, N_ADA * D_MODEL), 0.5 * D_MODEL ** -0.5)
    ada_b = nrm(ks[4], (DEPTH, N_ADA * D_MODEL), 0.02)
    norm_g = 1.0 + nrm(ks[5], (DEPTH, 3, D_MODEL), 0.02)
    ffn_w_in = nrm(ks[6], (DEPTH, 2, D_MODEL, 2 * D_FF), D_MODEL ** -0.5)
    ffn_w_out = nrm(ks[7], (DEPTH, 2, D_FF, D_MODEL), D_FF ** -0.5)
    mix_w_in = nrm(ks[8], (DEPTH, D_MODEL, IN_WIDTH), D_MODEL ** -0.5)
    gdn_conv_w = nrm(ks[9], (DEPTH, GDN_CONV, 3 * GDN_WIDTH), GDN_CONV ** -0.5)
    gdn_a_log = jnp.log(jax.random.uniform(ks[10], (DEPTH, GDN_HEADS), jnp.float32, 1.0, 16.0))
    dt = jnp.exp(jax.random.uniform(ks[11], (DEPTH, GDN_HEADS), jnp.float32, math.log(1e-3), math.log(1e-1)))
    gdn_dt_bias = dt + jnp.log(-jnp.expm1(-dt))
    gdn_norm_g = 1.0 + nrm(ks[12], (DEPTH, GDN_HEAD_DIM), 0.02)
    cmp_pe_k = nrm(ks[13], (DEPTH, CMP_LEN, NSA_HEAD_DIM), 0.1)
    cmp_w1_k = nrm(ks[14], (DEPTH, CMP_LEN * NSA_HEAD_DIM, CMP_HIDDEN), (CMP_LEN * NSA_HEAD_DIM) ** -0.5)
    cmp_w2_k = nrm(ks[15], (DEPTH, CMP_HIDDEN, NSA_HEAD_DIM), CMP_HIDDEN ** -0.5)
    cmp_pe_v = nrm(ks[16], (DEPTH, CMP_LEN, NSA_HEAD_DIM), 0.1)
    cmp_w1_v = nrm(ks[17], (DEPTH, CMP_LEN * NSA_HEAD_DIM, CMP_HIDDEN), (CMP_LEN * NSA_HEAD_DIM) ** -0.5)
    cmp_w2_v = nrm(ks[18], (DEPTH, CMP_HIDDEN, NSA_HEAD_DIM), CMP_HIDDEN ** -0.5)
    nsa_norm_g = 1.0 + nrm(ks[19], (DEPTH, NSA_HEAD_DIM), 0.02)
    mix_w_out = nrm(ks[20], (DEPTH, MIX_WIDTH, D_MODEL), MIX_WIDTH ** -0.5)
    final_norm_g = 1.0 + nrm(ks[21], (D_MODEL,), 0.02)
    return {"x": x, "c": c, "positions": positions, "ada_w": ada_w, "ada_b": ada_b,
            "norm_g": norm_g, "ffn_w_in": ffn_w_in, "ffn_w_out": ffn_w_out,
            "mix_w_in": mix_w_in, "gdn_conv_w": gdn_conv_w, "gdn_a_log": gdn_a_log,
            "gdn_dt_bias": gdn_dt_bias, "gdn_norm_g": gdn_norm_g,
            "cmp_pe_k": cmp_pe_k, "cmp_w1_k": cmp_w1_k, "cmp_w2_k": cmp_w2_k,
            "cmp_pe_v": cmp_pe_v, "cmp_w1_v": cmp_w1_v, "cmp_w2_v": cmp_w2_v,
            "nsa_norm_g": nsa_norm_g, "mix_w_out": mix_w_out, "final_norm_g": final_norm_g}

def first_block(x, c, positions, ada_w, ada_b, norm_g, ffn_w_in, ffn_w_out, mix_w_in,
              gdn_conv_w, gdn_a_log, gdn_dt_bias, gdn_norm_g, cmp_pe_k, cmp_w1_k, cmp_w2_k,
              cmp_pe_v, cmp_w1_v, cmp_w2_v, nsa_norm_g, mix_w_out, final_norm_g):
    B, T, D = x.shape
    half = ROT_DIM // 2
    inv_freq = jnp.power(ROPE_THETA, -jnp.arange(half, dtype=jnp.float32) * (2.0 / ROT_DIM))
    ang = positions.astype(jnp.float32)[..., None] * inv_freq
    cos = jnp.cos(ang)[:, :, None, :]
    sin = jnp.sin(ang)[:, :, None, :]
    cond = jax.nn.silu(c.astype(jnp.float32))
    for l in range(DEPTH):
        mod = (cond @ ada_w[l].astype(jnp.float32) + ada_b[l].astype(jnp.float32)).reshape(B, 3, 3, D).astype(x.dtype)
        h = modulate(rms_norm(x, norm_g[l, 0]), mod[:, 0, 0], mod[:, 0, 1])
        x = x + 0.5 * mod[:, 0, 2][:, None, :] * swiglu(h, ffn_w_in[l, 0], ffn_w_out[l, 0])
        h = modulate(rms_norm(x, norm_g[l, 1]), mod[:, 1, 0], mod[:, 1, 1])
        y = token_mix(h, mix_w_in[l], gdn_conv_w[l], gdn_a_log[l], gdn_dt_bias[l], gdn_norm_g[l],
                      cmp_pe_k[l], cmp_w1_k[l], cmp_w2_k[l], cmp_pe_v[l], cmp_w1_v[l], cmp_w2_v[l],
                      nsa_norm_g[l], mix_w_out[l], cos, sin)
        x = x + mod[:, 1, 2][:, None, :] * y.astype(x.dtype)
        h = modulate(rms_norm(x, norm_g[l, 2]), mod[:, 2, 0], mod[:, 2, 1])
        x = x + 0.5 * mod[:, 2, 2][:, None, :] * swiglu(h, ffn_w_in[l, 1], ffn_w_out[l, 1])
    return rms_norm(x, final_norm_g)


DEPTH_2 = 1

MLA_HEADS = 8
QK_NOPE = 64
QK_ROPE = 32
V_DIM = 64
Q_LORA = 384
KV_LORA = 256
ROPE_BASE = 10000.0
MLA_OUT = MLA_HEADS * V_DIM
RWKV_HEADS = 8
RWKV_HEAD = 64
RWKV_DIM = RWKV_HEADS * RWKV_HEAD
DECAY_LORA = 64
AAA_LORA = 64
GATE_LORA = 128
LNX_EPS = 64e-5
N_DIR = 2
N_BRANCH = 2
MLA_IN = Q_LORA + KV_LORA + QK_ROPE
RWKV_IN = 3 * RWKV_DIM + N_DIR * DECAY_LORA + N_DIR * AAA_LORA + GATE_LORA
GATE_IN = N_BRANCH * D_MODEL
IN_DIM = MLA_IN + RWKV_IN + GATE_IN
N_GROUPS = 4
EXPERTS_PER_GROUP = 8
N_EXPERTS = N_GROUPS * EXPERTS_PER_GROUP
TOP_K = 2
D_EXPERT = 256
MOE_BLOCK = 128


def rms_norm_2(x, g, eps=NORM_EPS):
    xf = x.astype(jnp.float32)
    y = xf * lax.rsqrt(jnp.mean(xf * xf, axis=-1, keepdims=True) + eps)
    return (y * g.astype(jnp.float32)).astype(x.dtype)

def apply_rope(x, cos, sin):
    half = x.shape[-1] // 2
    x1 = x[..., :half].astype(jnp.float32)
    x2 = x[..., half:].astype(jnp.float32)
    out = jnp.concatenate([x1 * cos - x2 * sin, x1 * sin + x2 * cos], axis=-1)
    return out.astype(x.dtype)

def mla_branch(z, q_norm_g, kv_norm_g, w_uq, w_ukv):
    B, S, _ = z.shape
    c_q = rms_norm_2(z[..., :Q_LORA], q_norm_g)
    c_kv = rms_norm_2(z[..., Q_LORA:Q_LORA + KV_LORA], kv_norm_g)
    k_rope = z[..., Q_LORA + KV_LORA:]
    q = (c_q @ w_uq).reshape(B, S, MLA_HEADS, QK_NOPE + QK_ROPE)
    kv = (c_kv @ w_ukv).reshape(B, S, MLA_HEADS, QK_NOPE + V_DIM)
    q_nope, q_rope = q[..., :QK_NOPE], q[..., QK_NOPE:]
    k_nope, v = kv[..., :QK_NOPE], kv[..., QK_NOPE:]
    pos = jnp.arange(S, dtype=jnp.float32)
    inv_freq = ROPE_BASE ** (-jnp.arange(0, QK_ROPE, 2, dtype=jnp.float32) / QK_ROPE)
    ang = pos[:, None] * inv_freq[None, :]
    cos, sin = jnp.cos(ang), jnp.sin(ang)
    q_rope = apply_rope(q_rope, cos[:, None, :], sin[:, None, :])
    k_rope = apply_rope(k_rope, cos, sin)
    scale = (QK_NOPE + QK_ROPE) ** -0.5
    nb = S // Q_BLOCK
    qn_b = q_nope.reshape(B, nb, Q_BLOCK, MLA_HEADS, QK_NOPE).transpose(1, 0, 2, 3, 4)
    qr_b = q_rope.reshape(B, nb, Q_BLOCK, MLA_HEADS, QK_ROPE).transpose(1, 0, 2, 3, 4)

    def attend(blk):
        qn, qr = blk
        s = (jnp.einsum('bqhd,bkhd->bhqk', qn, k_nope)
             + jnp.einsum('bqhd,bkd->bhqk', qr, k_rope))
        p = jax.nn.softmax(s.astype(jnp.float32) * scale, axis=-1).astype(v.dtype)
        return jnp.einsum('bhqk,bkhd->bqhd', p, v)

    o = lax.map(attend, (qn_b, qr_b))
    return o.transpose(1, 0, 2, 3, 4).reshape(B, S, MLA_OUT)

def token_shift_centred(z, mu_prev, mu_next):
    z_prev = jnp.pad(z[:, :-1], ((0, 0), (1, 0), (0, 0)))
    z_next = jnp.pad(z[:, 1:], ((0, 0), (0, 1), (0, 0)))
    return z + mu_prev * (z_prev - z) + mu_next * (z_next - z)

def wkv7_scan(r, w, k, v, a_vec, b_vec):
    B, S, H, N = r.shape

    def step(state, inp):
        r_t, w_t, k_t, v_t, a_t, b_t = inp
        sa = jnp.einsum('bhvk,bhk->bhv', state, a_t)
        state = (state * w_t[:, :, None, :] + sa[..., None] * b_t[:, :, None, :]
                 + v_t[..., None] * k_t[:, :, None, :])
        return state, jnp.einsum('bhvk,bhk->bhv', state, r_t)

    xs = tuple(jnp.moveaxis(t, 1, 0) for t in (r, w, k, v, a_vec, b_vec))
    s0 = jnp.zeros((B, H, N, N), jnp.float32)
    _, y = lax.scan(step, s0, xs)
    return jnp.moveaxis(y, 0, 1)

def rwkv_branch(z, mu_prev, mu_next, w0, w_up, a0, a_up, g_up, k_k, k_a, r_k, lnx_g, lnx_b):
    B, S, _ = z.shape
    C, H, N = RWKV_DIM, RWKV_HEADS, RWKV_HEAD
    f32 = jnp.float32
    zf = token_shift_centred(z.astype(f32), mu_prev.astype(f32), mu_next.astype(f32))
    r, k, v = zf[..., :C], zf[..., C:2 * C], zf[..., 2 * C:3 * C]
    o = 3 * C
    wd = zf[..., o:o + N_DIR * DECAY_LORA].reshape(B, S, N_DIR, DECAY_LORA)
    o += N_DIR * DECAY_LORA
    ad = zf[..., o:o + N_DIR * AAA_LORA].reshape(B, S, N_DIR, AAA_LORA)
    o += N_DIR * AAA_LORA
    gd = zf[..., o:]
    w_logit = w0.astype(f32) + jnp.einsum('bsdr,drc->bsdc', jnp.tanh(wd), w_up.astype(f32))
    decay = jnp.exp(-jnp.exp(-jax.nn.softplus(-w_logit) - 0.5))
    a = jax.nn.sigmoid(a0.astype(f32) + jnp.einsum('bsdr,drc->bsdc', ad, a_up.astype(f32)))
    g = jax.nn.sigmoid(gd) @ g_up.astype(f32)

    def heads(t):
        return t.reshape(t.shape[:-1] + (H, N))

    kk = heads(k * k_k.astype(f32))
    kk = kk / jnp.maximum(jnp.sqrt(jnp.sum(kk * kk, axis=-1, keepdims=True)), 1e-12)
    k_dir = heads(k[:, :, None, :] * (1.0 + (a - 1.0) * k_a.astype(f32)))
    a_h, decay_h = heads(a), heads(decay)
    r_h, v_h = heads(r), heads(v)
    y_f = wkv7_scan(r_h, decay_h[:, :, 0], k_dir[:, :, 0], v_h, -kk, kk * a_h[:, :, 0])
    fl = lambda t: jnp.flip(t, axis=1)
    y_b = fl(wkv7_scan(fl(r_h), fl(decay_h[:, :, 1]), fl(k_dir[:, :, 1]), fl(v_h),
                       fl(-kk), fl(kk * a_h[:, :, 1])))
    y = y_f + y_b
    mu = jnp.mean(y, axis=-1, keepdims=True)
    var = jnp.mean(jnp.square(y - mu), axis=-1, keepdims=True)
    y = ((y - mu) * lax.rsqrt(var + LNX_EPS)).reshape(B, S, C)
    y = y * lnx_g.astype(f32) + lnx_b.astype(f32)
    bonus = jnp.sum(r_h[:, :, None] * k_dir * heads(r_k.astype(f32)), axis=-1, keepdims=True) * v_h[:, :, None]
    y = y + jnp.sum(bonus, axis=2).reshape(B, S, C)
    return (y * g).astype(z.dtype)

def hier_moe(h, rg_w, rg_b, re_w, re_b, w1, w3, w2):
    B, S, D = h.shape
    T = B * S
    ht = h.reshape(T, D)
    group_p = jax.nn.softmax((ht @ rg_w + rg_b).astype(jnp.float32), axis=-1)
    gp, gi = lax.top_k(group_p, 1)
    gp, gi = gp[:, 0], gi[:, 0]
    e_logits = (ht @ re_w + re_b).astype(jnp.float32).reshape(T, N_GROUPS, EXPERTS_PER_GROUP)
    sel = jnp.take_along_axis(e_logits, gi[:, None, None], axis=1)[:, 0]
    ep = jax.nn.softmax(sel, axis=-1)
    tp, ti = lax.top_k(ep, TOP_K)
    tp = tp / jnp.sum(tp, axis=-1, keepdims=True)
    weight = gp[:, None] * tp
    expert = gi[:, None] * EXPERTS_PER_GROUP + ti
    A = T * TOP_K
    flat_e = expert.reshape(A)
    flat_w = weight.reshape(A)
    flat_tok = jnp.repeat(jnp.arange(T, dtype=jnp.int32), TOP_K)
    order = jnp.argsort(flat_e)
    se, stok, sw = flat_e[order], flat_tok[order], flat_w[order]
    counts = jnp.bincount(flat_e, length=N_EXPERTS)
    padded = ((counts + MOE_BLOCK - 1) // MOE_BLOCK) * MOE_BLOCK
    start = jnp.cumsum(counts) - counts
    pend = jnp.cumsum(padded)
    pstart = pend - padded
    dest = pstart[se] + (jnp.arange(A, dtype=jnp.int32) - start[se])
    n_blocks = -(-A // MOE_BLOCK) + N_EXPERTS
    cap = n_blocks * MOE_BLOCK
    slot_tok = jnp.full((cap,), T, jnp.int32).at[dest].set(stok)
    slot_w = jnp.zeros((cap,), h.dtype).at[dest].set(sw.astype(h.dtype))
    block_e = jnp.minimum(jnp.searchsorted(pend, jnp.arange(n_blocks) * MOE_BLOCK, side='right'),
                          N_EXPERTS - 1)
    h_pad = jnp.concatenate([ht, jnp.zeros((1, D), ht.dtype)], axis=0)
    xb = h_pad[slot_tok].reshape(n_blocks, MOE_BLOCK, D)

    def expert_block(args):
        xblk, e = args
        hid = jax.nn.silu(xblk @ w1[e]) * (xblk @ w3[e])
        return hid @ w2[e]

    yb = lax.map(expert_block, (xb, block_e)).reshape(cap, D)
    y = jax.ops.segment_sum(yb * slot_w[:, None], slot_tok, num_segments=T + 1)[:T]
    return y.reshape(B, S, D)

def second_inputs(seed: int = 0) -> dict:
    key = jax.random.key(seed)
    ks = iter(jax.random.split(key, 48))
    L, D, C = DEPTH_2, D_MODEL, RWKV_DIM
    f32 = jnp.float32
    nrm = lambda shape, s: jax.random.normal(next(ks), shape, f32) * s
    uni = lambda shape, lo, hi: jax.random.uniform(next(ks), shape, f32, lo, hi)
    return {
        'x': nrm((BATCH, SEQ, D), 1.0),
        'norm_mix_g': 1.0 + nrm((L, D), 0.02),
        'w_in': nrm((L, D, IN_DIM), D ** -0.5),
        'q_norm_g': 1.0 + nrm((L, Q_LORA), 0.02),
        'kv_norm_g': 1.0 + nrm((L, KV_LORA), 0.02),
        'w_uq': nrm((L, Q_LORA, MLA_HEADS * (QK_NOPE + QK_ROPE)), Q_LORA ** -0.5),
        'w_ukv': nrm((L, KV_LORA, MLA_HEADS * (QK_NOPE + V_DIM)), KV_LORA ** -0.5),
        'w_br_mla': nrm((L, MLA_OUT, D), MLA_OUT ** -0.5),
        'mu_prev': uni((L, RWKV_IN), 0.0, 0.5),
        'mu_next': uni((L, RWKV_IN), 0.0, 0.5),
        'w0': uni((L, N_DIR, C), -3.0, 1.0),
        'w_up': nrm((L, N_DIR, DECAY_LORA, C), 0.5 * DECAY_LORA ** -0.5),
        'a0': nrm((L, N_DIR, C), 0.1),
        'a_up': nrm((L, N_DIR, AAA_LORA, C), 0.5 * AAA_LORA ** -0.5),
        'g_up': nrm((L, GATE_LORA, C), GATE_LORA ** -0.5),
        'k_k': 0.85 + nrm((L, C), 0.02),
        'k_a': 1.0 + nrm((L, C), 0.02),
        'r_k': nrm((L, C), 0.1),
        'lnx_g': 1.0 + nrm((L, C), 0.02),
        'lnx_b': nrm((L, C), 0.01),
        'w_br_rwkv': nrm((L, C, D), C ** -0.5),
        'gate_b': nrm((L, N_BRANCH, D), 0.01),
        'w_out': nrm((L, D, D), D ** -0.5),
        'norm_ffn_g': 1.0 + nrm((L, D), 0.02),
        'router_group_w': nrm((L, D, N_GROUPS), D ** -0.5),
        'router_group_b': nrm((L, N_GROUPS), 0.01),
        'router_expert_w': nrm((L, D, N_EXPERTS), D ** -0.5),
        'router_expert_b': nrm((L, N_EXPERTS), 0.01),
        'w1': nrm((L, N_EXPERTS, D, D_EXPERT), D ** -0.5),
        'w3': nrm((L, N_EXPERTS, D, D_EXPERT), D ** -0.5),
        'w2': nrm((L, N_EXPERTS, D_EXPERT, D), D_EXPERT ** -0.5),
        'norm_final_g': 1.0 + nrm((D,), 0.02),
    }

def second_block(x, norm_mix_g, w_in, q_norm_g, kv_norm_g, w_uq, w_ukv, w_br_mla,
              mu_prev, mu_next, w0, w_up, a0, a_up, g_up, k_k, k_a, r_k, lnx_g, lnx_b,
              w_br_rwkv, gate_b, w_out, norm_ffn_g, router_group_w, router_group_b,
              router_expert_w, router_expert_b, w1, w3, w2, norm_final_g):
    B, S, D = x.shape
    for l in range(DEPTH_2):
        h = rms_norm_2(x, norm_mix_g[l])
        z = h @ w_in[l]
        z_mla = z[..., :MLA_IN]
        z_rwkv = z[..., MLA_IN:MLA_IN + RWKV_IN]
        z_gate = z[..., MLA_IN + RWKV_IN:].reshape(B, S, N_BRANCH, D)
        o_mla = mla_branch(z_mla, q_norm_g[l], kv_norm_g[l], w_uq[l], w_ukv[l])
        o_rwkv = rwkv_branch(z_rwkv, mu_prev[l], mu_next[l], w0[l], w_up[l], a0[l], a_up[l],
                             g_up[l], k_k[l], k_a[l], r_k[l], lnx_g[l], lnx_b[l])
        gates = jax.nn.sigmoid(z_gate + gate_b[l])
        mixed = gates[:, :, 0] * (o_mla @ w_br_mla[l]) + gates[:, :, 1] * (o_rwkv @ w_br_rwkv[l])
        x = x + mixed @ w_out[l]
        h2 = rms_norm_2(x, norm_ffn_g[l])
        x = x + hier_moe(h2, router_group_w[l], router_group_b[l], router_expert_w[l],
                         router_expert_b[l], w1[l], w3[l], w2[l])
    return rms_norm_2(x, norm_final_g)


def setup_inputs(seed=0):
    out = dict(first_inputs(seed))
    for name, value in second_inputs(seed + 1).items():
        if name != "x":
            out[name + "_2"] = value
    return out


def reference(
    x, c, positions, ada_w, ada_b, norm_g, ffn_w_in, ffn_w_out, mix_w_in, gdn_conv_w, gdn_a_log,
    gdn_dt_bias, gdn_norm_g, cmp_pe_k, cmp_w1_k, cmp_w2_k, cmp_pe_v, cmp_w1_v, cmp_w2_v,
    nsa_norm_g, mix_w_out, final_norm_g, norm_mix_g_2, w_in_2, q_norm_g_2, kv_norm_g_2, w_uq_2,
    w_ukv_2, w_br_mla_2, mu_prev_2, mu_next_2, w0_2, w_up_2, a0_2, a_up_2, g_up_2, k_k_2, k_a_2,
    r_k_2, lnx_g_2, lnx_b_2, w_br_rwkv_2, gate_b_2, w_out_2, norm_ffn_g_2, router_group_w_2,
    router_group_b_2, router_expert_w_2, router_expert_b_2, w1_2, w3_2, w2_2, norm_final_g_2,
):
    x = first_block(
        x, c, positions, ada_w, ada_b, norm_g, ffn_w_in, ffn_w_out, mix_w_in, gdn_conv_w,
        gdn_a_log, gdn_dt_bias, gdn_norm_g, cmp_pe_k, cmp_w1_k, cmp_w2_k, cmp_pe_v, cmp_w1_v,
        cmp_w2_v, nsa_norm_g, mix_w_out, final_norm_g,
    )
    return second_block(
        x, norm_mix_g_2, w_in_2, q_norm_g_2, kv_norm_g_2, w_uq_2, w_ukv_2, w_br_mla_2,
        mu_prev_2, mu_next_2, w0_2, w_up_2, a0_2, a_up_2, g_up_2, k_k_2, k_a_2, r_k_2, lnx_g_2,
        lnx_b_2, w_br_rwkv_2, gate_b_2, w_out_2, norm_ffn_g_2, router_group_w_2,
        router_group_b_2, router_expert_w_2, router_expert_b_2, w1_2, w3_2, w2_2,
        norm_final_g_2,
    )


_drawn_inputs = setup_inputs


def setup_inputs(seed=0):
    import zlib

    import numpy as np

    out = dict(_drawn_inputs(seed))
    spreads = {}
    factors = {'gdn_norm_g': 4.202,
     'cmp_pe_k': 4.237,
     'nsa_norm_g': 3.153,
     'norm_mix_g_2': 3.089,
     'q_norm_g_2': 8.0,
     'kv_norm_g_2': 4.82,
     'k_k_2': 25.93,
     'k_a_2': 2.877,
     'lnx_g_2': 43.56,
     'lnx_b_2': 58.6,
     'gate_b_2': 24.249,
     'router_expert_b_2': 51.6,
     'norm_final_g_2': 7.913,
     'norm_ffn_g_2': 8.0,
     'router_group_b_2': 8.0}
    for name, (base, spread) in spreads.items():
        noise = np.random.default_rng([zlib.crc32(name.encode()), seed]).standard_normal(out[name].shape)
        drawn = base * np.exp(spread * noise) if base else spread * noise
        out[name] = __import__('jax').numpy.asarray(drawn.astype(out[name].dtype))
    for name, factor in factors.items():
        out[name] = (out[name] * factor).astype(out[name].dtype)
    return out
```

```python
from contextlib import ExitStack

import numpy as np
import concourse.bass as bass
from concourse import mybir

F32 = mybir.dt.float32
I32 = mybir.dt.int32
ALU = mybir.AluOpType
ACT = mybir.ActivationFunctionType
AX_X = mybir.AxisListType.X

P = 128
D = 1024
KT = D // P
T = 256
TT = T // P
DEPTH = 2
D_FF = 2816
FT = D_FF // P
GDN_H = 4
NSA_R = 4
CMP_LEN, CMP_STRIDE = 32, 16
N_CMP = (T - CMP_LEN) // CMP_STRIDE + 1
N_EXP, N_GRP, D_EXP = 32, 4, 256
ET = N_EXP * D_EXP // P
EPS = 1e-6
LNX_EPS = 64e-5
KAPPA = float(np.exp(np.float32(-0.5)))
BIG = 1e30
RING = 12
CHUNK = 1024
ADA = 72
ADA_BLOCK = ADA // 3
FFN = 3 * FT
MIX = 27
INV_LEVELS = 7
GATES_EARLY = 7

STREAM = {}
_at = 0
STREAM["ada"] = _at
_at += ADA_BLOCK
for _l in range(DEPTH):
    for _name, _n in (("ffn0", FFN), ("mix", MIX), ("cmp", 8), ("mixout", 8), ("ffn1", FFN)):
        STREAM[_name, _l] = _at
        _at += _n
for _name, _n in (("mla", 6), ("uq", 3), ("ukv", 3), ("rwkv", 15), ("gate", GATES_EARLY), ("up", 2), ("gate_late", 16 - GATES_EARLY),
                  ("br_mla", 4), ("br_rwkv", 4), ("out", 8), ("moe", 3 * ET)):
    STREAM[_name] = _at
    _at += _n
N_CHUNKS = _at

ADA_CALLS = ((0, 0, 1), (0, 1, 2), (1, 0, 1), (1, 1, 2))
BESIDE = (("ffn0", 0), ("ffn1", 0), ("ffn0", 1))
ADA_PAIRS = ADA_BLOCK // 2


def pairs_before(call):
    return ADA_PAIRS * sum(n for _, _, n in ADA_CALLS[1:call])


PARAMS = {}
_at = 0
for _name, _n in (
    ("c", KT), ("ada_b", DEPTH * ADA), ("norm_g", DEPTH * 3 * KT), ("conv_w", DEPTH * 12 * 4),
    ("a_log", DEPTH * GDN_H), ("dt_bias", DEPTH * GDN_H), ("gdn_norm_g", DEPTH), ("nsa_norm_g", DEPTH),
    ("pe_k", DEPTH * CMP_LEN), ("pe_v", DEPTH * CMP_LEN), ("w2_k", DEPTH * P), ("w2_v", DEPTH * 64),
    ("final_g", KT), ("norm_mix_g", KT), ("q_norm_g", 3), ("kv_norm_g", 2), ("mu_prev", 15), ("mu_next", 15),
    ("w0", 8), ("a0", 8), ("k_k", 4), ("k_a", 4), ("r_k", 4), ("lnx_g", 4), ("lnx_b", 4), ("gate_b", 16),
    ("norm_ffn_g", KT), ("router_w", KT * 36), ("router_b", 36), ("norm_final_g", KT),
):
    PARAMS[_name] = (_at, _n)
    _at += _n
N_PARAMS = _at

CONSTS = {}
_at = 0
for _name, _n in (
    ("ident", P), ("ones", P), ("mean_d", P), ("mean_gdn", P), ("block_ones", P), ("block_mean", P),
    ("mean_q", P), ("mean_kv", P), ("triu", P), ("cum_mask", P), ("strict", P), ("perm_nsa", P), ("perm_mla", P),
    ("ones_column", 2 * RING - 1), ("inv_freq", 1), ("eps", 1), ("lnx_eps", 1), ("half_pi", 1), ("one", 1),
    ("causal", TT * T), ("cmp_mask", TT * 16), ("iota", 36),
    ("inv_masks", 2 * INV_LEVELS * P), ("cos_mla", T), ("sin_mla", T), ("wkv_masks", 2 * 3 * P),
):
    CONSTS[_name] = (_at, _n)
    _at += _n
N_CONSTS = _at


def constants():
    f = np.float32
    i, j = np.arange(P)[:, None], np.arange(P)[None, :]
    t = {}
    t["ident"] = (i == j)
    t["ones"] = np.ones((P, P))
    t["mean_d"] = np.full((P, P), 1.0 / D)
    t["mean_gdn"] = np.full((P, P), 1.0 / P)
    t["block_ones"] = (i // 64 == j // 64)
    t["block_mean"] = (i // 64 == j // 64) / 64.0
    t["mean_q"] = np.full((P, P), 1.0 / 384)
    t["mean_kv"] = np.full((P, P), 1.0 / 256)
    t["triu"] = (i <= j)
    t["cum_mask"] = np.where(i <= j, 0.0, -BIG)
    t["strict"] = (i < j)
    for name, block in (("perm_nsa", 64), ("perm_mla", 32)):
        half = 8 if block == 64 else 16
        m = np.zeros((P, P))
        for b in range(0, P, block) if block == 64 else (64,):
            for n in range(half):
                m[b + half + n, b + n] = -1.0
                m[b + n, b + half + n] = 1.0
        t[name] = m
    d = np.arange(P) % 64
    freq = np.power(f(500000.0), -np.arange(8, dtype=f) * f(2.0 / 16)).astype(f)
    t["ones_column"] = np.broadcast_to(np.arange(2 * RING - 1) == RING - 1, (P, 2 * RING - 1))
    t["inv_freq"] = np.where(d < 16, freq[d % 8], f(0.0))[:, None]
    t["eps"] = np.full((P, 1), EPS)
    t["lnx_eps"] = np.full((P, 1), LNX_EPS)
    t["half_pi"] = np.full((P, 1), np.pi / 2)
    t["one"] = np.ones((P, 1))
    q = np.arange(T).reshape(TT, P).T[:, :, None]
    t["causal"] = np.where(np.arange(T)[None, None, :] <= q, 0.0, -BIG)
    end = np.arange(16) * CMP_STRIDE + CMP_LEN - 1
    t["cmp_mask"] = np.where((end <= q) & (np.arange(16) < N_CMP), 0.0, -BIG)
    t["iota"] = np.broadcast_to(np.arange(36), (P, 36))
    masks = []
    for direction in range(2):
        for level in range(INV_LEVELS):
            b = 1 << level
            m = (i // (2 * b) == j // (2 * b)) & (i // b % 2 == 0) & (j // b % 2 == 1)
            masks.append(m if direction == 0 else m.T)
    t["inv_masks"] = np.stack(masks, 1)
    freq = np.power(f(10000.0), -np.arange(0, 32, 2, dtype=f) / f(32))[np.arange(P) % 16][:, None]
    ang = np.where(i // 32 == 2, freq * np.arange(T, dtype=f)[None, :], f(0.0)).astype(f)
    t["cos_mla"], t["sin_mla"] = np.cos(ang), np.sin(ang)
    t["wkv_masks"] = np.stack([i <= j, i < j, i <= j, i >= j, i > j, i >= j], 1)
    return np.concatenate([np.asarray(t[n], f).reshape(P, -1) for n in CONSTS], 1)


def pack(x):
    f = np.float32

    def col_tiles(w):
        k, n = w.shape
        return w.reshape(k // P, P, n // P, P).transpose(2, 1, 0, 3).reshape(n // P, P, k)

    stream = np.zeros((N_CHUNKS + DEPTH * ADA - ADA_BLOCK, P, CHUNK), f)

    def put(at, chunks):
        stream[at:at + len(chunks)] = chunks

    def swiglu(at, gate, up, down):
        n = len(gate)
        g = np.array([0] + [2 + 3 * i for i in range(n - 1)])
        o = np.array([4 + 3 * i for i in range(n - 1)] + [3 * n - 1])
        stream[at + g], stream[at + g + 1], stream[at + o] = gate, up, down

    nsa_q = np.array([g * 256 + r * 64 + d for r in range(4) for g in range(2) for d in range(64)])
    ada = np.concatenate([col_tiles(x["ada_w"][l]) for l in range(DEPTH)])
    put(STREAM["ada"], ada[:ADA_BLOCK])
    put(N_CHUNKS, ada[ADA_BLOCK:])
    for l in range(DEPTH):
        for i in range(2):
            w = x["ffn_w_in"][l, i]
            swiglu(STREAM[f"ffn{i}", l], col_tiles(w[:, :D_FF]), col_tiles(w[:, D_FF:]),
                   x["ffn_w_out"][l, i].reshape(FT, P, D))
        w = x["mix_w_in"][l]
        kv = 2568
        cols = [w[:, 0:2048], w[:, 2056:2568][:, nsa_q]]
        cols += [w[:, kv + n * P:kv + (n + 1) * P] for n in (0, 2, 4, 1, 3, 5)]
        cols += [w[:, 2048:2056], w[:, 3336:3360], np.zeros((D, 96), f)]
        put(STREAM["mix", l], col_tiles(np.concatenate(cols, 1)))
        for n, w1 in enumerate((x["cmp_w1_v"][l], x["cmp_w1_k"][l])):
            w1 = w1.reshape(4, 8, 64, P).transpose(0, 2, 1, 3).reshape(4, 64, CHUNK)
            put(STREAM["cmp", l] + 4 * n, np.concatenate([w1, w1], 1))
        w = x["mix_w_out"][l]
        put(STREAM["mixout", l], col_tiles(np.concatenate([w[:512], w[512:][nsa_q]], 0)))
    w = x["w_in_2"][0]
    put(STREAM["mla"], col_tiles(np.concatenate([w[:, 0:640], np.zeros((D, 64), f), w[:, 640:672], np.zeros((D, 32), f)], 1)))
    put(STREAM["rwkv"], col_tiles(w[:, 672:2592]))
    put(STREAM["gate"], col_tiles(w[:, 2592:])[:GATES_EARLY])
    put(STREAM["gate_late"], col_tiles(w[:, 2592:])[GATES_EARLY:])
    w = np.pad(x["w_uq_2"][0].reshape(3, P, 8, 96), ((0, 0), (0, 0), (0, 0), (0, 32)))
    put(STREAM["uq"], w.transpose(1, 2, 0, 3).reshape(P, 3, CHUNK).transpose(1, 0, 2))
    w = x["w_ukv_2"][0].reshape(2, P, 8, 128)
    kn = np.pad(w[..., :64], ((0, 0), (0, 0), (0, 0), (0, 64))).transpose(1, 2, 0, 3)
    put(STREAM["ukv"], kn.reshape(P, 2, CHUNK).transpose(1, 0, 2))
    put(STREAM["ukv"] + 2, w[..., 64:].reshape(2, P, 512).transpose(1, 0, 2).reshape(1, P, CHUNK))
    wa = np.concatenate([x["w_up_2"][0].reshape(P, 512), x["a_up_2"][0].reshape(P, 512)], 1)
    gu = np.concatenate([x["g_up_2"][0], np.zeros((P, 512), f)], 1)
    put(STREAM["up"], np.stack([wa, gu]))
    for name, w in (("br_mla", x["w_br_mla_2"][0]), ("br_rwkv", x["w_br_rwkv_2"][0])):
        put(STREAM[name], w.reshape(4, P, 4, 2, P).transpose(2, 1, 3, 0, 4).reshape(4, P, CHUNK))
    put(STREAM["out"], col_tiles(x["w_out_2"][0]))
    experts = [np.concatenate([col_tiles(x[n][0, e]) for e in range(N_EXP)]) for n in ("w1_2", "w3_2")]
    swiglu(STREAM["moe"], experts[0], experts[1], x["w2_2"][0].reshape(ET, P, D))

    def feat(v):
        return np.ascontiguousarray(v).reshape(-1, P).T

    def rows(v):
        return np.broadcast_to(np.ascontiguousarray(v).reshape(1, -1), (P, v.size))

    two = lambda v: np.concatenate([v, v], -1)
    p = {
        "c": feat(x["c"]), "ada_b": feat(x["ada_b"]), "norm_g": feat(x["norm_g"]),
        "conv_w": x["gdn_conv_w"].reshape(DEPTH, 4, 12, P).transpose(3, 0, 2, 1),
        "a_log": rows(x["gdn_a_log"]), "dt_bias": rows(x["gdn_dt_bias"]),
        "gdn_norm_g": feat(x["gdn_norm_g"]), "nsa_norm_g": feat(two(x["nsa_norm_g"])),
        "pe_k": feat(two(x["cmp_pe_k"])), "pe_v": feat(two(x["cmp_pe_v"])),
        "w2_k": two(x["cmp_w2_k"]).transpose(1, 0, 2), "w2_v": x["cmp_w2_v"].transpose(1, 0, 2),
        "final_g": feat(x["final_norm_g"]), "norm_mix_g": feat(x["norm_mix_g_2"]),
        "q_norm_g": feat(x["q_norm_g_2"]), "kv_norm_g": feat(x["kv_norm_g_2"]),
        "mu_prev": feat(x["mu_prev_2"]), "mu_next": feat(x["mu_next_2"]),
        "w0": feat(x["w0_2"]), "a0": feat(x["a0_2"]), "k_k": feat(x["k_k_2"]), "k_a": feat(x["k_a_2"]),
        "r_k": feat(x["r_k_2"]), "lnx_g": feat(x["lnx_g_2"]), "lnx_b": feat(x["lnx_b_2"]),
        "gate_b": feat(x["gate_b_2"]), "norm_ffn_g": feat(x["norm_ffn_g_2"]),
        "router_w": np.concatenate([x["router_group_w_2"][0], x["router_expert_w_2"][0]], 1)
                      .reshape(KT, P, 36).transpose(1, 0, 2),
        "router_b": rows(np.concatenate([x["router_group_b_2"][0], x["router_expert_b_2"][0]])),
        "norm_final_g": feat(x["norm_final_g_2"]),
    }
    params = np.concatenate([np.asarray(p[n], f).reshape(P, -1) for n in PARAMS], 1)
    assert params.shape == (P, N_PARAMS)
    x_t = x["x"].reshape(T, KT, P).transpose(2, 1, 0)
    pos = np.broadcast_to(x["positions"].reshape(1, T).astype(np.int32), (P, T))
    return {"weights": stream, "params": params, "consts": constants(),
            "x_t": np.ascontiguousarray(x_t), "pos": np.ascontiguousarray(pos)}


def build(nc, weights, params, consts, x_t, pos, out):
    ctx = ExitStack()
    sems = {}

    def S(name):
        if name not in sems:
            sems[name] = ctx.enter_context(nc.semaphore(name))
        return sems[name]

    def sb(name, shape, dt=F32):
        return ctx.enter_context(nc.sbuf_tensor(name, shape, dt))

    ring = sb("ring", [P, RING, 8, P])
    par = sb("par", [P, N_PARAMS])
    cst = sb("cst", [P, N_CONSTS])
    xt = sb("xt", [P, KT, T])
    h = sb("h", [P, KT, T])
    sq = sb("sq", [P, KT, T])
    std = sb("std", [P, T])
    rstd = sb("rstd", [P, T])
    mod = sb("mod", [P, ADA])
    mod_a = sb("mod_a", [P, 3, KT])
    mod_g = sb("mod_g", [P, 3, KT])
    cond = sb("cond", [P, KT, 2 * RING - 1])
    ada_rows = sb("ada_rows", [RING, 2 * ADA_BLOCK // RING, P])
    cos_t = sb("cos_t", [P, T])
    sin_t = sb("sin_t", [P, T])
    zeros = sb("zeros", [1, 512])
    silu_gate = sb("silu_gate", [P, 2, T])
    hidden = sb("hidden", [P, 2, T])
    hid_raw = sb("hid_raw", [P, 2, T])
    arena = sb("arena", [P, 23700])
    ada_pair = arena[:, 0:4 * CHUNK].rearrange("p (s a k n) -> p s a k n", s=2, a=2, n=P)
    ada_scaled = arena[:, 4 * CHUNK:6 * CHUNK].rearrange("p (a k n) -> p a k n", a=2, n=P)
    ada_acc = arena[:, 6 * CHUNK:6 * CHUNK + 2 * ADA_BLOCK * P].rearrange("p (j n) -> p j n", n=P)
    cond_chunk = cond[:, :, RING - 1].unsqueeze(1).unsqueeze(3).broadcast_to((P, 2, KT, P))
    ps = ctx.enter_context(nc.psum_tensor("ps", [P, 8, 512], F32))

    def bank(b, *dims):
        v = ps[:, b, :]
        if len(dims) == 2:
            return v[:, 0:dims[0] * dims[1]].rearrange("p (a b) -> p a b", b=dims[1])
        if len(dims) == 3:
            return v[:, 0:dims[0] * dims[1] * dims[2]].rearrange("p (a b c) -> p a b c", b=dims[1], c=dims[2])
        return v[:, 0:dims[0]] if dims else v

    def const(name, *dims):
        at, n = CONSTS[name]
        v = cst[:, at:at + n]
        if len(dims) == 2:
            return v.rearrange("p (a b) -> p a b", b=dims[1])
        return v

    def param(name, at=0, n=None):
        first, width = PARAMS[name]
        return par[:, first + at:first + at + (width if n is None else n)]

    ident, ones, block_ones = const("ident"), const("ones"), const("block_ones")
    eps_c = const("eps")
    landed = [S(f"chunk_landed{i}") for i in range(RING)]

    def chunk(i):
        return ring[:, i % RING]

    def wait_chunk(eng, i, turn=0):
        eng.wait_ge(landed[i % RING], 16 * (i // RING + 1) + 16 * turn)

    class Steps:

        def __init__(self, eng, name):
            self.eng, self.sem, self.n = eng, S(name), 0

        def __call__(self, ins):
            self.n += 1
            ins.then_inc(self.sem, 1)
            self.eng.wait_ge(self.sem, self.n)

    steps = {}

    def own(eng, name):
        if name not in steps:
            steps[name] = Steps(eng, name)
        return steps[name]

    def bc(v, n, axis=1):
        shape = list(v.shape)
        shape.insert(axis, n)
        return v.unsqueeze(axis).broadcast_to(tuple(shape))

    def setup_act(act):
        act.dma_start(par[:, :], params).then_inc(S("tables_loaded"), 16)
        act.dma_start(cst[:, :], consts).then_inc(S("tables_loaded"), 16)
        act.dma_start(xt[:, :, :], x_t).then_inc(S("x_loaded"), 16)
        act.dma_start(arena[:, 0:T].bitcast(I32), pos).then_inc(S("pos_loaded"), 16)
        act.wait_ge(S("tables_loaded"), 32)
        act.wait_ge(S("zeroed"), 2)
        act.activation(cond[:, :, RING - 1], param("c"), ACT.Silu).then_inc(S("cond_ready"), 1)
        act.wait_ge(S("angle_ready"), 2)
        act.activation(sin_t[:, :], arena[:, 2 * T:3 * T], ACT.Sin)
        act.activation(cos_t[:, :], arena[:, 3 * T:4 * T], ACT.Sin).then_inc(S("rope_ready"), 1)

    def setup_dve(dve):
        own_dve = own(dve, "dve_step")
        dve.memset(zeros[:, :], 0.0).then_inc(S("zeroed"), 1)
        dve.memset(cond[:, :, :], 0.0).then_inc(S("zeroed"), 1)
        dve.wait_ge(S("tables_loaded"), 32)
        dve.wait_ge(S("pos_loaded"), 16)
        ang, pf = arena[:, T:2 * T], arena[:, 4 * T:5 * T]
        own_dve(dve.tensor_copy(pf, arena[:, 0:T].bitcast(I32)))
        own_dve(dve.tensor_scalar(ang, pf, const("inv_freq"), None, ALU.mult))
        two_pi = 2 * np.pi
        c1 = float(np.float32(6.28125))
        c2 = float(np.float32(two_pi - c1))
        c3 = float(two_pi - c1 - c2)
        turns, turns_i, near = arena[:, 5 * T:6 * T], arena[:, 6 * T:7 * T].bitcast(I32), arena[:, 7 * T:8 * T]
        for n, shift in enumerate((0.0, 0.25)):
            r = arena[:, (2 + n) * T:(3 + n) * T]
            own_dve(dve.tensor_scalar(turns, ang, 1.0 / two_pi, shift, ALU.mult, ALU.add))
            own_dve(dve.tensor_copy(turns_i, turns))
            own_dve(dve.tensor_copy(near, turns_i))
            own_dve(dve.scalar_tensor_tensor(r, near, -c1, ang, ALU.mult, ALU.add))
            own_dve(dve.scalar_tensor_tensor(r, near, -c2, r, ALU.mult, ALU.add))
            own_dve(dve.scalar_tensor_tensor(r, near, -c3, r, ALU.mult, ALU.add))
            own_dve(dve.tensor_scalar(r, r, shift * two_pi, None, ALU.add))
            own_dve(dve.tensor_scalar(turns, r, float(np.pi), -two_pi, ALU.is_gt, ALU.mult))
            own_dve(dve.tensor_tensor(r, r, turns, ALU.add))
            own_dve(dve.tensor_scalar(turns, r, -float(np.pi), two_pi, ALU.is_lt, ALU.mult))
            own_dve(dve.tensor_tensor(r, r, turns, ALU.add))
            lim = float(np.float32(3.1415925))
            dve.tensor_scalar(r, r, lim, -lim, ALU.min, ALU.max).then_inc(S("angle_ready"), 1)
        dve.wait_ge(S("rope_ready"), 1)

    def stream_sp(sp):
        for s in range(RING):
            sp.dma_start(ring[:, s], weights[s].rearrange("p (k n) -> p k n", n=P)).then_inc(landed[s], 16)
        turns = N_CHUNKS // RING
        with sp.Fori(1, turns) as turn:
            for s in range(RING):
                sp.wait_ge(S("chunk_used"), RING * turn + (s + 1 - RING))
                sp.dma_start(ring[:, s], weights[bass.ds(RING * turn + s, 1)].rearrange("a p (k n) -> p (a k) n", n=P))\
                  .then_inc(landed[s], 16)
        for i in range(turns * RING, N_CHUNKS):
            sp.wait_ge(S("chunk_used"), i + 1 - RING)
            sp.dma_start(chunk(i), weights[i].rearrange("p (k n) -> p k n", n=P)).then_inc(landed[i % RING], 16)

    def ada_group(g):
        return ps[0:RING, 7, g * P:(g + 1) * P]

    def ada_groups(call):
        return ADA_CALLS[call][2] * ADA_BLOCK // RING

    def ada_first_pe(pe):
        pe.wait_ge(S("cond_ready"), 1)
        pe.wait_ge(S("zeroed"), 2)
        for i in range(ADA_BLOCK):
            j = i % RING
            wait_chunk(pe, STREAM["ada"] + i)
            for k in range(KT):
                mm = pe.matmul(ada_group(i // RING), cond[:, k, RING - 1 - j:2 * RING - 1 - j], chunk(STREAM["ada"] + i)[:, k],
                               start=(j == 0 and k == 0), stop=(j == RING - 1 and k == KT - 1))
            mm.then_inc(S("chunk_used"), 1)

    def ada_sums_pe(pe, call, half):
        n = ada_groups(call) // 2
        pe.wait_ge(S("ada_reduced"), pairs_before(call + 1))
        for g in range(half * n, (half + 1) * n):
            for j in range(RING):
                mm = pe.matmul(ada_group(g), const("ones_column")[:, RING - 1 - j:2 * RING - 1 - j],
                               ada_acc[:, g * RING + j], start=(j == 0), stop=(j == RING - 1))
        mm.then_inc(S("ada_sums"), 1)

    def ada_columns_pe(pe, call):
        pe.wait_ge(S("ada_evac"), call + 1)
        n = ada_groups(call)
        for g in range(n):
            mm = pe.transpose(bank(4, n, RING)[:, g], ada_rows[:, g, :], ident[0:RING, 0:RING])
        mm.then_inc(S("ada_columns"), 1)

    def ada_pool(pool, call):
        per = ADA_CALLS[call][2]
        first = N_CHUNKS + 2 * pairs_before(call)
        if call == 1:
            pool.wait_ge(S("rope_ready"), 1)
        else:
            pool.wait_ge(S("x_ready"), call)
        for s in range(per):
            pool.dma_start(ada_pair[:, s].rearrange("p a k n -> p a (k n)"),
                           weights[first + 2 * s:first + 2 * s + 2].rearrange("a p n -> p a n"))\
                .then_inc(S(f"ada_landed{s}"), 16)
        with pool.Fori(1, ADA_PAIRS) as turn:
            for s in range(per):
                pool.wait_ge(S("ada_scaled"), turn * per + (pairs_before(call) + s + 1 - per))
                pool.dma_start(ada_pair[:, s].rearrange("p a k n -> p a (k n)"),
                               weights[bass.ds(turn * (2 * per) + (first + 2 * s), 2)].rearrange("a p n -> p a n"))\
                    .then_inc(S(f"ada_landed{s}"), 16)

    def ada_pair_dve(dve, call, q, turn=None):
        per, before = ADA_CALLS[call][2], pairs_before(call)
        at = 0 if turn is None else turn
        s = q % per
        held = ADA_PAIRS * sum(n > s for _, _, n in ADA_CALLS[1:call])
        dve.wait_ge(S(f"ada_landed{s}"), 16 * at + 16 * (held + q // per + 1))
        if before + q > 0:
            dve.wait_ge(S("ada_reduced"), at * per + (before + q))
        dve.tensor_tensor(ada_scaled[:, :, :, :], ada_pair[:, s], cond_chunk, ALU.mult).then_inc(S("ada_scaled"), 1)
        dve.wait_ge(S("ada_scaled"), at * per + (before + q + 1))
        into = ada_acc[:, 2 * q:2 * q + 2] if turn is None else ada_acc[:, bass.ds(turn * (2 * per) + 2 * q, 2)]
        dve.tensor_reduce(into, ada_scaled.rearrange("p a k n -> p a n k"), AX_X, ALU.add).then_inc(S("ada_reduced"), 1)

    def ada_dve(dve, call):
        own_dve = own(dve, "dve_step")
        l, first, blocks = ADA_CALLS[call]
        n = ada_groups(call)
        if call == 0:
            dve.wait_ge(S("chunk_used"), STREAM["ada"] + ADA_BLOCK)
        else:
            dve.wait_ge(S("ada_sums"), 2 * call)
        dve.tensor_copy(ada_rows[:, 0:n, :].rearrange("p a n -> p (a n)"), ps[0:RING, 7, 0:n * P]).then_inc(S("ada_evac"), 1)
        dve.wait_ge(S("ada_columns"), call + 1)
        at, width = first * ADA_BLOCK, blocks * ADA_BLOCK
        own_dve(dve.tensor_tensor(mod[:, at:at + width], bank(4, width), param("ada_b", l * ADA + at, width), ALU.add))
        for i in range(first, first + blocks):
            scale = mod[:, (3 * i + 1) * KT:(3 * i + 2) * KT]
            gain = param("norm_g", (3 * l + i) * KT, KT)
            dve.scalar_tensor_tensor(mod_a[:, i, :], scale, 1.0, gain, ALU.add, ALU.mult)
            gate = mod[:, (3 * i + 2) * KT:(3 * i + 3) * KT]
            last = dve.tensor_scalar(mod_g[:, i, :], gate, 1.0 if i == 1 else 0.5, None, ALU.mult)
        last.then_inc(S("mod_ready"), 1)
        dve.wait_ge(S("mod_ready"), call + 1)

    def norm_act(act, n):
        if n == 0:
            act.wait_ge(S("x_loaded"), 16)
        else:
            act.wait_ge(S("x_ready"), n)
        act.activation(sq[:, :, :], xt[:, :, :], ACT.Square).then_inc(S("sq_ready"), 1)
        act.wait_ge(S("ms_ready"), n + 1)
        act.activation(std[:, :], bank(6, T), ACT.Sqrt, bias=eps_c).then_inc(S("std_ready"), 1)

    def norm_pe(pe, n):
        pe.wait_ge(S("sq_ready"), n + 1)
        for k in range(KT):
            mm = pe.matmul(bank(6, T), const("mean_d"), sq[:, k], start=(k == 0), stop=(k == KT - 1))
        mm.then_inc(S("ms_ready"), 1)

    def norm_dve(dve, n, gain, shift=None, into=None, ada_call=None):
        own_dve = own(dve, "dve_step")
        into = h if into is None else into
        dve.wait_ge(S("std_ready"), n + 1)
        own_dve(dve.reciprocal(rstd[:, :], std[:, :]))
        own_dve(dve.tensor_tensor(into[:, :, :], xt[:, :, :], bc(rstd[:, :], KT), ALU.mult))
        if ada_call is not None:
            ada_dve(dve, ada_call)
        for k in range(KT):
            if shift is None:
                last = dve.tensor_scalar(into[:, k], into[:, k], gain[:, k:k + 1], None, ALU.mult)
            else:
                last = dve.tensor_scalar(into[:, k], into[:, k], gain[:, k:k + 1], shift[:, k:k + 1], ALU.mult, ALU.add)
        last.then_inc(S("h_ready") if into is h else S("x_ready"), 1)

    def ffN_CHUNKS(first, f, n):
        gate = first + (0 if f == 0 else 3 * f - 1)
        return gate, gate + 1, first + (3 * n - 1 if f == n - 1 else 4 + 3 * f)

    def ffn_pe(pe, n, first, base, h_count):
        pe.wait_ge(S("h_ready"), h_count)
        per = RING // 3

        def up(f, turn=0):
            gate, value, _ = ffN_CHUNKS(first, f, n)
            for half, i in enumerate((gate, value)):
                wait_chunk(pe, i, turn)
                for k in range(KT):
                    mm = pe.matmul(bank(4 + f % 2, 2, T)[:, half], chunk(i)[:, k], h[:, k],
                                   start=(k == 0), stop=(k == KT - 1))
                mm.then_inc(S("chunk_used"), 1)

        def down(f, turn=0):
            i = ffN_CHUNKS(first, f, n)[2]
            wait_chunk(pe, i, turn)
            for k in range(KT):
                mm = pe.matmul(bank(k // 2, 2, T)[:, k % 2], chunk(i)[:, k], hidden[:, f % 2],
                               start=False, stop=(f == n - 1), skip_group_check=True)
            mm.then_inc(S("chunk_used"), 1)

        for b in range(4):
            pe.matmul(bank(b), zeros[:, 0:P], zeros[:, :], start=True, stop=False, skip_group_check=True)
        up(0)
        turns = (n - 1) // per
        with pe.Fori(0, turns) as turn:
            for s in range(per):
                up(s + 1, turn)
                pe.wait_ge(S("hidden_ready"), turn * per + (base + s + 1))
                down(s, turn)
        for s in range(turns * per, n - 1):
            up(s + 1)
            pe.wait_ge(S("hidden_ready"), base + s + 1)
            down(s)
        pe.wait_ge(S("hidden_ready"), base + n)
        down(n - 1)

    def ffn_act(act, n, first, base):
        def gate(f, turn=None):
            at = 0 if turn is None else turn
            act.wait_ge(S("chunk_used"), 6 * at + ffN_CHUNKS(first, f, n)[1] + 1)
            if f >= 2:
                act.wait_ge(S("hidden_ready"), 2 * at + (base + f - 1))
            act.activation(silu_gate[:, f % 2], bank(4 + f % 2, 2, T)[:, 0], ACT.Silu).then_inc(S("silu_ready"), 1)

        gate(0)
        gate(1)
        with act.Fori(0, (n - 2) // 2) as turn:
            gate(2, turn)
            gate(3, turn)

    def ffn_dve(dve, n, first, base, gate_col, weight=None, ada_call=None):
        def product(f, turn=None):
            at = 0 if turn is None else turn
            dve.wait_ge(S("silu_ready"), 2 * at + (base + f + 1))
            if f >= 2:
                dve.wait_ge(S("chunk_used"), 6 * at + ffN_CHUNKS(first, f - 2, n)[2] + 1)
            up = bank(4 + f % 2, 2, T)[:, 1]
            if weight is None:
                dve.tensor_tensor(hidden[:, f % 2], silu_gate[:, f % 2], up, ALU.mult).then_inc(S("hidden_ready"), 1)
                return
            dve.tensor_tensor(hid_raw[:, f % 2], silu_gate[:, f % 2], up, ALU.mult).then_inc(S("hid_raw"), 1)
            dve.wait_ge(S("hid_raw"), 2 * at + (f + 1))
            w = weight[:, f // 2, :] if turn is None else weight[:, bass.ds(turn + f // 2, 1), :].rearrange("p a t -> p (a t)")
            dve.tensor_tensor(hidden[:, f % 2], hid_raw[:, f % 2], w, ALU.mult).then_inc(S("hidden_ready"), 1)

        if weight is not None:
            dve.wait_ge(S("weight_rows"), N_EXP // 2)
        per = 0 if ada_call is None else ADA_CALLS[ada_call][2]
        product(0)
        for q in range(per):
            ada_pair_dve(dve, ada_call, q)
        product(1)
        for q in range(per, 2 * per):
            ada_pair_dve(dve, ada_call, q)
        with dve.Fori(0, (n - 2) // 2) as turn:
            product(2, turn)
            if per:
                ada_pair_dve(dve, ada_call, 2 * per, turn)
            product(3, turn)
            if per == 2:
                ada_pair_dve(dve, ada_call, 2 * per + 1, turn)
        dve.wait_ge(S("chunk_used"), first + 3 * n)
        for k in range(KT):
            into = bank(k // 2, 2, T)[:, k % 2]
            if gate_col is None:
                last = dve.tensor_tensor(xt[:, k], into, xt[:, k], ALU.add)
            else:
                last = dve.scalar_tensor_tensor(xt[:, k], into, gate_col[:, k:k + 1], xt[:, k], ALU.mult, ALU.add)
        last.then_inc(S("x_ready"), 1)

    def place(at, *dims):
        n = int(np.prod(dims))
        v = arena[:, at:at + n]
        names = "abcd"[:len(dims)]
        if len(dims) == 1:
            return v
        return v.rearrange(f"p ({' '.join(names)}) -> p {' '.join(names)}", **dict(zip(names[1:], dims[1:])))

    inv_x, inv_xt, inv_p1 = place(0, 2, 4, P), place(1024, 2, 4, P), place(2048, 2, 4, P)
    inv_lt, inv_lb = place(9252, 2, 4, P), place(10276, 2, 4, P)
    inv_masks = const("inv_masks", 2 * INV_LEVELS, P)

    def inv_pool(pool, call, direction, lt_ready):
        base = 2 * INV_LEVELS * call
        for level in range(INV_LEVELS):
            for b in range(2):
                if level == 0:
                    pool.wait_ge(S("lt_ready"), lt_ready - 1 + b)
                elif level == 1:
                    pool.wait_ge(S("x_updated"), base + b + 1)
                else:
                    pool.wait_ge(S("p1_done"), base + 2 * (level - 1) + b + 1)
                pool.tensor_tensor(inv_lb[:, b], inv_lt[:, b], bc(inv_masks[:, direction * INV_LEVELS + level], 4),
                                   ALU.mult).then_inc(S("lb_ready"), 1)

    def inv_pe(pe, call):
        base = 2 * INV_LEVELS * call
        base_xx = 2 * (INV_LEVELS - 1) * call
        for b in range(2):
            pe.wait_ge(S("lb_ready"), base + b + 1)
            for i in range(4):
                mm = pe.transpose(bank(b, 4, P)[:, i], inv_lb[:, b, i], ident)
            mm.then_inc(S("p1_done"), 1)
        for level in range(1, INV_LEVELS):
            for b in range(2):
                pe.wait_ge(S("lb_ready"), base + 2 * level + b + 1)
                pe.wait_ge(S("x_updated"), base + 2 * (level - 1) + b + 1)
                for i in range(4):
                    mm = pe.matmul(bank(b, 4, P)[:, i], inv_lb[:, b, i], inv_x[:, b, i], start=True, stop=True)
                mm.then_inc(S("p1_done"), 1)
            for b in range(2):
                pe.wait_ge(S("p1_ready"), base_xx + 2 * (level - 1) + b + 1)
                if level < INV_LEVELS - 1:
                    for i in range(4):
                        pe.matmul(bank(2 + b, 4, P)[:, i], inv_xt[:, b, i], inv_p1[:, b, i], start=True, stop=True)
                for i in range(4):
                    mm = pe.matmul(bank(4 + b, 4, P)[:, i], inv_p1[:, b, i], inv_xt[:, b, i], start=True, stop=True)
                mm.then_inc(S("xp_done"), 1)

    def inv_act(act, call):
        base = 2 * INV_LEVELS * call
        base_xx = 2 * (INV_LEVELS - 1) * call
        for level in range(1, INV_LEVELS):
            for b in range(2):
                act.wait_ge(S("p1_done"), base + 2 * level + b + 1)
                act.activation(inv_p1[:, b], bank(b, 4, P), ACT.Copy).then_inc(S("p1_ready"), 1)

    def inv_dve(dve, call):
        base = 2 * INV_LEVELS * call
        base_xx = 2 * (INV_LEVELS - 1) * call
        for b in range(2):
            dve.wait_ge(S("p1_done"), base + b + 1)
            dve.tensor_tensor(inv_x[:, b], bc(ident, 4), bank(b, 4, P), ALU.subtract)
            dve.tensor_tensor(inv_xt[:, b], bc(ident, 4), inv_lb[:, b], ALU.subtract).then_inc(S("x_updated"), 1)
        for level in range(1, INV_LEVELS):
            for b in range(2):
                dve.wait_ge(S("xp_done"), base_xx + 2 * (level - 1) + b + 1)
                if level < INV_LEVELS - 1:
                    dve.tensor_tensor(inv_x[:, b], inv_x[:, b], bank(2 + b, 4, P), ALU.subtract)
                dve.tensor_tensor(inv_xt[:, b], inv_xt[:, b], bank(4 + b, 4, P), ALU.subtract)\
                   .then_inc(S("x_updated"), 1)

    conv_in = place(0, 12, T + 3)
    rn = place(0, 4, 512)
    pz = place(3108, 12, T)
    qkv = place(6180, 12, T)
    dec, attn = place(11300, 2, 4, P), place(12324, 2, 4, P)
    beta_mask, decay_row = place(13348, 2, 4, P), place(14372, 4, P)
    k_tok, bv = place(14884, 4, P), place(15396, 2, 4, P)
    k_hat, q_hat = place(16420, 4, P), place(16932, 4, P)
    state, v_new, resid = place(17444, 4, P), place(17956, 2, 4, P), place(18980, 4, P)
    v_tok = place(19492, 2, TT, P)
    misc = place(20004, TT, 32)
    beta, gates = place(20068, TT, 4), place(20076, TT, 24)
    a_in, a_abs, a_exp, a_sp = (place(20124 + 8 * n, TT, 4) for n in range(4))
    log_a, neg_gc = place(20156, TT, 4), place(20164, TT, 4)
    ea, last_arg, last_dec = place(20172, 4), place(20176, 4), place(20180, 4)
    win_k, win_v = place(9252, CMP_LEN, 16), place(9764, CMP_LEN, 16)
    cmp_hid, cmp_hid_t = place(10276, 4, P), place(10788, 4, 16)
    k_cmp, v_cmp = place(20192, 16), place(20208, P)
    cmp_p, cmp_max, cmp_sum = place(10996, 16, 16), place(11252, 16), place(11268, 16)
    cmp_pt = place(15444, 16, P)
    at_s, at_p, at_pt = place(11300, 2, 2, T), place(12324, 2, 2, T), place(13348, 2, 4, P)
    at_max, at_neg, at_sum, at_fac = (place(14372 + 32 * n, 16, 2) for n in range(4))
    SCALE = 64.0 ** -0.5

    def mix_pe(pe, l):
        first = STREAM["mix", l]
        pe.wait_ge(S("h_ready"), 3 * l + 2)
        for j in range(MIX):
            pe.wait_ge(S("proj_evac"), MIX * l + max(j - 3, 0))
            wait_chunk(pe, first + j)
            w = chunk(first + j)
            if j < 24:
                for k in range(KT):
                    mm = pe.matmul(bank(4 + j % 4, T), w[:, k], h[:, k], start=(k == 0), stop=(k == KT - 1))
            else:
                n = 32 if j == 26 else P
                for t in range(TT):
                    for k in range(KT):
                        mm = pe.matmul(bank(4 + j % 4, TT, n)[:, t], h[:, k, t * P:(t + 1) * P], w[:, k, 0:n],
                                       start=(k == 0), stop=(k == KT - 1))
            mm.then_inc(S("chunk_used"), 1)
        pe.wait_ge(S("head_squared"), 3 * l + 1)
        for b in range(4):
            mm = pe.matmul(bank(b), ones, sq[:, 2 * b:2 * b + 2, :], start=True, stop=True)
        mm.then_inc(S("head_ms"), 1)
        pe.wait_ge(S("head_std"), 3 * l + 1)
        pe.wait_ge(S("proj_evac"), MIX * (l + 1))
        for b in range(4):
            n = 2 if b < 3 else 1
            mm = pe.matmul(bank(b, n, T), const("perm_nsa"), pz[:, 4 + 2 * b:4 + 2 * b + n, :], start=True, stop=True)
        mm.then_inc(S("rotated"), 1)
        compress_pe(pe, l)

    def compress_pe(pe, l):
        first = STREAM["cmp", l]
        for n, win in enumerate((win_v, win_k)):
            pe.wait_ge(S("windows_ready"), 2 * l + n + 1)
            for c in range(4):
                wait_chunk(pe, first + 4 * n + c)
                for g in range(2):
                    half = slice(64 * g, 64 * g + 64)
                    for i in range(8):
                        mm = pe.matmul(ps[0:16, 6 + g, (1 - n) * P:(2 - n) * P], win[half, 8 * c + i, :],
                                       chunk(first + 4 * n + c)[half, i], start=(c == 0 and i == 0), stop=(c == 3 and i == 7))
                mm.then_inc(S("chunk_used"), 1)
        pe.wait_ge(S("cmp_hid"), l + 1)
        for n in range(4):
            mm = pe.transpose(bank(5, 4, 16)[:, n], cmp_hid[0:16, n, :], ident[0:16, 0:16])
        mm.then_inc(S("cmp_hid_turned"), 1)
        pe.wait_ge(S("cmp_hid_t"), l + 1)
        pe.matmul(bank(6, 2, 16), param("w2_k", l * P, P), cmp_hid_t[:, 0:2, :], start=True, stop=True)
        for g in range(2):
            mm = pe.matmul(ps[0:16, 7, g * 64:g * 64 + 64], cmp_hid_t[:, 2 + g, :], param("w2_v", l * 64, 64),
                           start=True, stop=True)
        mm.then_inc(S("cmp_kv"), 1)

    def mix_act(act, l):
        first = STREAM["mix", l]
        for j in range(MIX):
            act.wait_ge(S("chunk_used"), first + j + 1)
            b = 4 + j % 4
            if j < 12:
                act.activation(conv_in[:, j, 3:T + 3], bank(b, T), ACT.Copy).then_inc(S("proj_evac"), 1)
            elif j < 24:
                act.activation(pz[:, j - 12], bank(b, T), ACT.Copy).then_inc(S("proj_evac"), 1)
            elif j < 26:
                act.activation(v_tok[:, j - 24], bank(b, TT, P), ACT.Copy).then_inc(S("proj_evac"), 1)
            else:
                act.activation(misc[:, :, :], bank(b, TT, 32), ACT.Copy).then_inc(S("proj_evac"), 1)
            if j in (9, 15, 21):
                n = (j - 9) // 6
                act.wait_ge(S("conv_done"), 3 * l + n + 1)
                act.activation(qkv[:, 4 * n:4 * n + 4], qkv[:, 4 * n:4 * n + 4], ACT.Silu).then_inc(S("qkv_ready"), 1)
            if j == 22:
                act.wait_ge(S("qkv_ready"), 3 * l + 2)
                act.activation(sq[:, :, :], qkv[:, 0:8], ACT.Square).then_inc(S("head_squared"), 1)
        act.wait_ge(S("proj_evac"), MIX * (l + 1))
        act.activation(pz[:, 0:4], pz[:, 0:4], ACT.Silu).then_inc(S("z_ready"), 1)
        act.activation(beta[:, :, :], misc[:, :, 0:4], ACT.Sigmoid)
        act.activation(gates[:, :, :], misc[:, :, 8:32], ACT.Sigmoid).then_inc(S("gates_ready"), 1)
        act.wait_ge(S("head_ms"), 3 * l + 1)
        act.activation(rn[:, :, :], ps[:, 0:4, :], ACT.Sqrt, bias=eps_c).then_inc(S("head_std"), 1)
        act.wait_ge(S("a_abs_ready"), l + 1)
        act.activation(a_exp[:, :, :], a_abs[:, :, :], ACT.Exp, scale=-1.0).then_inc(S("a_exp_ready"), 1)
        act.activation(ea, param("a_log", l * GDN_H, GDN_H), ACT.Exp)
        act.wait_ge(S("a_exp_ready"), l + 1)
        act.activation(a_sp[:, :, :], a_exp[:, :, :], ACT.Ln, bias=const("one")).then_inc(S("softplus_ready"), 1)
        act.wait_ge(S("chunk_used"), STREAM["cmp", l] + 8)
        for g in range(2):
            last = act.activation(cmp_hid[0:16, g:4:2, :], ps[0:16, 6 + g, 0:2 * P].rearrange("p (n j) -> p n j", j=P), ACT.Silu)
        last.then_inc(S("cmp_hid"), 1)
        act.wait_ge(S("cmp_hid_turned"), l + 1)
        act.activation(cmp_hid_t[:, :, :], bank(5, 4, 16), ACT.Copy).then_inc(S("cmp_hid_t"), 1)
        act.wait_ge(S("cmp_kv"), l + 1)
        for g in range(2):
            half = slice(64 * g, 64 * g + 64)
            act.activation(k_cmp[half, :], ps[half, 6, 16 * g:16 * g + 16], ACT.Copy)
        act.activation(v_cmp[0:16, :], ps[0:16, 7, 0:P], ACT.Copy).then_inc(S("cmp_ready"), 1)

    def mix_dve(dve, l):
        own_dve = own(dve, "dve_step")

        def windows(win, tile, pe_name):
            dve.memset(win[:, :, N_CMP:16], 0.0)
            for half in range(2):
                src = pz[:, tile, half * CMP_STRIDE:half * CMP_STRIDE + CMP_STRIDE * N_CMP].rearrange("p (n l) -> p l n", l=CMP_STRIDE)
                term = bc(param(pe_name, l * CMP_LEN + half * CMP_STRIDE, CMP_STRIDE), N_CMP, axis=2)
                last = dve.tensor_tensor(win[:, half * CMP_STRIDE:(half + 1) * CMP_STRIDE, 0:N_CMP], src, term, ALU.add)
            last.then_inc(S("windows_ready"), 1)

        own_dve(dve.memset(conv_in[:, :, 0:3], 0.0))
        for n in range(3):
            dve.wait_ge(S("proj_evac"), MIX * l + 4 * n + 4)
            for tap in range(4):
                for j in range(4 * n, 4 * n + 4):
                    w = param("conv_w", (l * 12 + j) * 4 + tap, 1)
                    if tap == 0:
                        last = dve.tensor_scalar(qkv[:, j], conv_in[:, j, 0:T], w, None, ALU.mult)
                    else:
                        last = dve.scalar_tensor_tensor(qkv[:, j], conv_in[:, j, tap:T + tap], w, qkv[:, j], ALU.mult, ALU.add)
                if tap < 3:
                    own_dve(last)
            last.then_inc(S("conv_done"), 1)
        dve.wait_ge(S("proj_evac"), MIX * (l + 1))
        own_dve(dve.tensor_tensor(a_in[:, :, :], misc[:, :, 4:8], bc(param("dt_bias", l * GDN_H, GDN_H), TT), ALU.add))
        own_dve(dve.tensor_scalar(a_abs[:, :, :], a_in[:, :, :], -1.0, None, ALU.mult))
        dve.tensor_tensor(a_abs[:, :, :], a_abs[:, :, :], a_in[:, :, :], ALU.max).then_inc(S("a_abs_ready"), 1)
        windows(win_v, 11, "pe_v")
        dve.wait_ge(S("head_std"), 3 * l + 1)
        own_dve(dve.reciprocal(rn[:, :, :], rn[:, :, :]))
        r = rn[:, :, :].rearrange("p a (b t) -> p (a b) t", t=T)
        dve.scalar_tensor_tensor(qkv[:, 0:4], r[:, 0:4], float(P) ** -0.5, qkv[:, 0:4], ALU.mult, ALU.mult)
        dve.tensor_tensor(qkv[:, 4:8], r[:, 4:8], qkv[:, 4:8], ALU.mult).then_inc(S("qk_normed"), 1)
        dve.wait_ge(S("rotated"), l + 1)
        rot = sq[:, 0:7, :]
        dve.tensor_tensor(rot, ps[:, 0:4, :].rearrange("p a (b t) -> p (a b) t", t=T)[:, 0:7], bc(sin_t[:, :], 7), ALU.mult)
        own_dve(dve.tensor_tensor(pz[:, 4:11], pz[:, 4:11], bc(cos_t[:, :], 7), ALU.mult))
        dve.tensor_tensor(pz[:, 4:11], pz[:, 4:11], rot, ALU.add).then_inc(S("rope_done"), 1)
        dve.wait_ge(S("rope_done"), l + 1)
        windows(win_k, 8, "pe_k")
        dve.wait_ge(S("softplus_ready"), l + 1)
        dve.wait_ge(S("gates_ready"), l + 1)
        own_dve(dve.scalar_tensor_tensor(a_sp[:, :, :], a_in[:, :, :], 0.0, a_sp[:, :, :], ALU.max, ALU.add))
        dve.scalar_tensor_tensor(log_a[:, :, :], a_sp[:, :, :], -1.0, bc(ea, TT), ALU.mult, ALU.mult).then_inc(S("decay_ready"), 1)

    GDN_BANKS = ((4, 5, 6, 7), (1, 2, 3, 0))

    def gdn_pe(pe, l):
        pe.wait_ge(S("decay_ready"), l + 1)
        pe.wait_ge(S("cmp_ready"), l + 1)
        pe.wait_ge(S("qk_normed"), l + 1)
        for c in range(TT):
            mm = pe.matmul(bank(0, TT, 4)[:, c], const("triu"), log_a[:, c, :], start=True, stop=True)
        mm.then_inc(S("gc_column"), 1)
        for c in range(TT):
            rows_b, beta_b, kk_b, qk_b = GDN_BANKS[c]
            tok = slice(c * P, (c + 1) * P)
            if c == 1:
                pe.wait_ge(S("neg_gc_ready"), l + 1)
            for hd in range(GDN_H):
                q, k = qkv[:, hd, tok], qkv[:, 4 + hd, tok]
                pe.matmul(bank(rows_b, 4, P)[:, hd], log_a[:, c, hd:hd + 1].broadcast_to((P, P)), const("triu"), start=True, stop=True)
                pe.matmul(bank(beta_b, 4, P)[:, hd], beta[:, c, hd:hd + 1].broadcast_to((P, P)), ident, start=True, stop=True)
                pe.matmul(bank(kk_b, 4, P)[:, hd], k, k, start=True, stop=True)
                mm = pe.matmul(bank(qk_b, 4, P)[:, hd], k, q, start=True, stop=True)
            mm.then_inc(S("gdn_products"), 1)
        pe.wait_ge(S("lt_ready"), gdn_lt(l) + 1)
        for c in range(TT):
            for hd in range(GDN_H):
                pe.transpose(bank(4 + c, 4, P)[:, hd], qkv[:, 8 + hd, c * P:(c + 1) * P], ident)
        for hd in range(GDN_H):
            mm = pe.transpose(bank(6, 4, P)[:, hd], qkv[:, 4 + hd, 0:P], ident)
        mm.then_inc(S("by_token"), 1)
        pe.wait_ge(S("gdn_operands"), l + 1)
        inv_pe(pe, l)
        pe.wait_ge(S("x_updated"), 2 * INV_LEVELS * (l + 1))
        for hd in range(GDN_H):
            mm = pe.matmul(bank(0, 4, P)[:, hd], inv_xt[:, 0, hd], bv[:, 0, hd], start=True, stop=True)
        mm.then_inc(S("v_new_done"), 1)
        pe.wait_ge(S("v_new_ready"), 2 * l + 1)
        for hd in range(GDN_H):
            mm = pe.matmul(bank(1, 4, P)[:, hd], k_tok[:, hd], v_new[:, 0, hd], start=True, stop=True)
        mm.then_inc(S("state_done"), 1)
        for hd in range(GDN_H):
            mm = pe.matmul(bank(2, 4, P)[:, hd], v_new[:, 0, hd], attn[:, 0, hd], start=True, stop=True)
        mm.then_inc(S("gdn_o_done"), 1)
        pe.wait_ge(S("state_ready"), l + 1)
        for hd in range(GDN_H):
            mm = pe.matmul(bank(3, 4, P)[:, hd], k_hat[:, hd], state[:, hd], start=True, stop=True)
        mm.then_inc(S("held_done"), 1)
        pe.wait_ge(S("resid_ready"), l + 1)
        for hd in range(GDN_H):
            mm = pe.matmul(bank(0, 4, P)[:, hd], inv_xt[:, 1, hd], resid[:, hd], start=True, stop=True)
        mm.then_inc(S("v_new_done"), 1)
        pe.wait_ge(S("v_new_ready"), 2 * l + 2)
        for hd in range(GDN_H):
            pe.matmul(bank(1, 4, P)[:, hd], state[:, hd], q_hat[:, hd], start=True, stop=False)
            mm = pe.matmul(bank(1, 4, P)[:, hd], v_new[:, 1, hd], attn[:, 1, hd], start=False, stop=True)
        mm.then_inc(S("gdn_o_done"), 1)
        pe.wait_ge(S("head_squared"), 3 * l + 2)
        for b in range(2):
            mm = pe.matmul(bank(2 + b), const("mean_gdn"), sq[:, 2 * b:2 * b + 2, :], start=True, stop=True)
        mm.then_inc(S("head_ms"), 1)

    def gdn_lt(l):
        return 2 * l

    def gdn_act(act, l):
        for c in range(TT):
            act.wait_ge(S("decay_arg"), 2 * l + c + 1)
            act.activation(dec[:, c], dec[:, c], ACT.Exp)
            if c == 0:
                last = act.activation(last_dec, last_arg, ACT.Exp)
            else:
                last = act.activation(decay_row[:, :, :], bank(GDN_BANKS[1][0], 4, P), ACT.Exp)
            last.then_inc(S("decay_exp"), 1)
        inv_act(act, l)
        for c in range(TT):
            act.wait_ge(S("v_new_done"), 2 * l + c + 1)
            act.activation(v_new[:, c], bank(0, 4, P), ACT.Copy).then_inc(S("v_new_ready"), 1)
            if c == 0:
                act.wait_ge(S("state_done"), l + 1)
                act.activation(state[:, :, :], bank(1, 4, P), ACT.Copy).then_inc(S("state_ready"), 1)
            act.wait_ge(S("gdn_o_done"), 2 * l + c + 1)
            act.activation(h[:, 0:4, c * P:(c + 1) * P], bank(2 - c, 4, P), ACT.Copy).then_inc(S("gdn_o_ready"), 1)
        act.wait_ge(S("gdn_o_ready"), 2 * l + 2)
        act.activation(sq[:, 0:4, :], h[:, 0:4, :], ACT.Square).then_inc(S("head_squared"), 1)
        act.wait_ge(S("head_ms"), 3 * l + 2)
        act.activation(rn[:, 0:2, :], ps[:, 2:4, :], ACT.Sqrt, bias=eps_c).then_inc(S("head_std"), 1)

    def gdn_dve(dve, l):
        own_dve = own(dve, "dve_step")
        dve.wait_ge(S("gc_column"), l + 1)
        dve.tensor_scalar(neg_gc[:, :, :], bank(0, TT, 4), -1.0, None, ALU.mult).then_inc(S("neg_gc_ready"), 1)
        dve.wait_ge(S("neg_gc_ready"), l + 1)

        def decay_args(c):
            rows_b, beta_b, _, _ = GDN_BANKS[c]
            dve.wait_ge(S("gdn_products"), 2 * l + c + 1)
            for hd in range(GDN_H):
                last = dve.scalar_tensor_tensor(dec[:, c, hd], bank(rows_b, 4, P)[:, hd], neg_gc[:, c, hd:hd + 1],
                                                const("cum_mask"), ALU.add, ALU.add)
            if c == 0:
                last = dve.tensor_tensor(last_arg, bank(rows_b, 4, P)[:, :, P - 1], neg_gc[:, 0, :], ALU.add)
            last.then_inc(S("decay_arg"), 1)
            own_dve(dve.tensor_tensor(beta_mask[:, c], bank(beta_b, 4, P), bc(const("strict"), 4), ALU.mult))

        def matrices(c):
            _, _, kk_b, qk_b = GDN_BANKS[c]
            dve.wait_ge(S("decay_exp"), 2 * l + c + 1)
            dve.tensor_tensor(attn[:, c], bank(qk_b, 4, P), dec[:, c], ALU.mult)
            own_dve(dve.tensor_tensor(inv_lt[:, c], bank(kk_b, 4, P), dec[:, c], ALU.mult))
            dve.tensor_tensor(inv_lt[:, c], inv_lt[:, c], beta_mask[:, c], ALU.mult).then_inc(S("lt_ready"), 1)

        decay_args(0)
        decay_args(1)
        matrices(0)
        matrices(1)
        own_dve(dve.tensor_tensor(k_hat[:, :, :], qkv[:, 4:8, P:T], bank(GDN_BANKS[1][1], 4, P), ALU.mult))
        dve.tensor_tensor(k_hat[:, :, :], k_hat[:, :, :], decay_row[:, :, :], ALU.mult)
        dve.tensor_tensor(q_hat[:, :, :], qkv[:, 0:4, P:T], decay_row[:, :, :], ALU.mult)
        dve.wait_ge(S("by_token"), l + 1)
        for c in range(TT):
            dve.tensor_tensor(bv[:, c], bank(4 + c, 4, P), bc(beta[:, c, :], P, axis=2), ALU.mult)
        dve.tensor_tensor(k_tok[:, :, :], bank(6, 4, P), bc(last_dec, P, axis=2), ALU.mult).then_inc(S("gdn_operands"), 1)
        inv_dve(dve, l)
        dve.wait_ge(S("held_done"), l + 1)
        dve.tensor_tensor(resid[:, :, :], bv[:, 1], bank(3, 4, P), ALU.subtract).then_inc(S("resid_ready"), 1)
        dve.wait_ge(S("head_std"), 3 * l + 2)
        dve.wait_ge(S("z_ready"), l + 1)
        own_dve(dve.reciprocal(rn[:, 0:2, :], rn[:, 0:2, :]))
        own_dve(dve.tensor_tensor(h[:, 0:4], h[:, 0:4], rn[:, 0:2, :].rearrange("p a (b t) -> p (a b) t", t=T), ALU.mult))
        dve.scalar_tensor_tensor(h[:, 0:4], h[:, 0:4], param("gdn_norm_g", l, 1), pz[:, 0:4], ALU.mult, ALU.mult)\
           .then_inc(S("y_ready"), 1)

    def at_step(i):
        return i // 8, i % 8 // 2, i % 2

    def nsa_pe(pe, l):
        base = 16 * l
        pe.wait_ge(S("cmp_ready"), l + 1)
        pe.wait_ge(S("rope_done"), l + 1)
        pe.wait_ge(S("y_ready"), 2 * l + 1)
        for i in range(16):
            qt, r, g = at_step(i)
            half = slice(64 * g, 64 * g + 64)
            mm = pe.matmul(bank(6 + g, 8, 16)[:, i // 2], pz[half, 4 + r, qt * P:(qt + 1) * P], k_cmp[half, :], start=True, stop=True)
        mm.then_inc(S("cmp_scores"), 1)
        pe.wait_ge(S("cmp_p_ready"), l + 1)
        for i in range(16):
            mm = pe.transpose(ps[0:16, 2 + i // 4, (i % 4) * P:(i % 4 + 1) * P], cmp_p[:, i, :], ident)
        mm.then_inc(S("cmp_p_turned"), 1)
        pe.wait_ge(S("cmp_pt_ready"), l + 1)
        for i in range(16 + 2):
            if i < 16:
                qt, r, g = at_step(i)
                half, nk = slice(64 * g, 64 * g + 64), (qt + 1) * P
                if i >= 2:
                    pe.wait_ge(S("at_arg"), base + i - 1)
                for b in range(2):
                    mm = pe.matmul(bank(i % 2, 2, T)[:, b, 0:nk], pz[half, 4 + r, qt * P:(qt + 1) * P], pz[half, 9 + b, 0:nk],
                                   start=True, stop=True)
                mm.then_inc(S("at_scores"), 1)
            if 1 <= i <= 16:
                j = i - 1
                pe.wait_ge(S("at_p"), base + j + 1)
                if j >= 2:
                    pe.wait_ge(S("at_pt"), base + j - 1)
                for b in range(2):
                    for t in range(j // 8 + 1):
                        mm = pe.transpose(bank(2 + j % 2, 4, P)[:, 2 * b + t], at_p[:, j % 2, b, t * P:(t + 1) * P], ident)
                mm.then_inc(S("at_turned"), 1)
            if i >= 2:
                j = i - 2
                pe.wait_ge(S("at_pt"), base + j + 1)
                if j >= 2:
                    pe.wait_ge(S("at_y"), base + j - 1)
                half = slice(64 * (j % 2), 64 * (j % 2) + 64)
                o = ps[half, 4 + j % 2, 0:P]
                pe.matmul(o, v_cmp[0:16, half], cmp_pt[0:16, j, :], start=True, stop=False)
                for b in range(2):
                    for t in range(j // 8 + 1):
                        mm = pe.matmul(o, v_tok[:, b, t, half], at_pt[:, j % 2, 2 * b + t], start=False, stop=(b == 1 and t == j // 8))
                mm.then_inc(S("at_o"), 1)
        pe.wait_ge(S("head_squared"), 3 * l + 3)
        for b in range(2):
            mm = pe.matmul(bank(6 + b), const("block_mean"), sq[:, 4 + 2 * b:6 + 2 * b, :], start=True, stop=True)
        mm.then_inc(S("head_ms"), 1)

    def nsa_act(act, l):
        base = 16 * l
        act.wait_ge(S("cmp_arg"), l + 1)
        act.activation(cmp_p[:, :, :], cmp_p[:, :, :], ACT.Exp, scale=SCALE).then_inc(S("cmp_exp"), 1)
        act.wait_ge(S("cmp_p_turned"), l + 1)
        act.activation(cmp_pt[0:16].rearrange("p (a b) t -> p a (b t)", b=4), ps[0:16, 2:6, :], ACT.Copy).then_inc(S("cmp_pt_ready"), 1)
        for i in range(16 + 2):
            if i < 16:
                nk = (i // 8 + 1) * P
                act.wait_ge(S("at_arg"), base + i + 1)
                if i >= 2:
                    act.wait_ge(S("at_turned"), base + i - 1)
                for b in range(2):
                    e = act.activation(at_p[:, i % 2, b, 0:nk], at_s[:, i % 2, b, 0:nk], ACT.Exp, bias=at_neg[:, i, b:b + 1],
                                       scale=SCALE, accum_out=at_sum[:, i, b:b + 1])
                e.then_inc(S("at_exp"), 1)
            if 1 <= i <= 16:
                j = i - 1
                act.wait_ge(S("at_turned"), base + j + 1)
                if j >= 2:
                    act.wait_ge(S("at_o"), base + j - 1)
                n = j // 8 + 1
                src = bank(2 + j % 2, 2, 2 * P)[:, :, 0:n * P]
                act.activation(at_pt[:, j % 2].rearrange("p (b t) q -> p b (t q)", b=2)[:, :, 0:n * P], src, ACT.Copy)\
                   .then_inc(S("at_pt"), 1)
            if i >= 2:
                j = i - 2
                qt, r, g = at_step(j)
                half = slice(64 * g, 64 * g + 64)
                act.wait_ge(S("at_o"), base + j + 1)
                act.activation(h[half, 4 + r, qt * P:(qt + 1) * P], ps[half, 4 + j % 2, 0:P], ACT.Copy).then_inc(S("at_y"), 1)
        act.wait_ge(S("at_y"), base + 16)
        act.activation(sq[:, 4:8, :], h[:, 4:8, :], ACT.Square).then_inc(S("head_squared"), 1)
        act.wait_ge(S("head_ms"), 3 * l + 3)
        act.activation(rn[:, 2:4, :], ps[:, 6:8, :], ACT.Sqrt, bias=eps_c).then_inc(S("head_std"), 1)

    def nsa_dve(dve, l):
        own_dve = own(dve, "dve_step")
        base = 16 * l
        dve.wait_ge(S("cmp_scores"), l + 1)
        for g in range(2):
            last = dve.tensor_tensor(cmp_p.rearrange("p (t r g) c -> p g t r c", t=TT, g=2)[:, g], bank(6 + g, TT, 4, 16),
                                     bc(const("cmp_mask", TT, 16), 4, axis=2), ALU.add)
        own_dve(last)
        own_dve(dve.tensor_reduce(cmp_max, cmp_p[:, :, :], AX_X, ALU.max))
        own_dve(dve.tensor_scalar(cmp_max, cmp_max, -BIG / 10, None, ALU.max))
        dve.tensor_tensor(cmp_p[:, :, :], cmp_p[:, :, :], bc(cmp_max, 16, axis=2), ALU.subtract).then_inc(S("cmp_arg"), 1)
        dve.wait_ge(S("cmp_exp"), l + 1)
        own_dve(dve.tensor_reduce(cmp_sum, cmp_p[:, :, :], AX_X, ALU.add))
        own_dve(dve.tensor_scalar(cmp_sum, cmp_sum, 1e-30, None, ALU.max))
        own_dve(dve.reciprocal(cmp_sum, cmp_sum))
        for t in range(TT):
            fac = cmp_sum[:, 8 * t:8 * t + 8].rearrange("p (r g) -> p r g", g=2)
            gate = gates[:, t, :].rearrange("p (g r b) -> p r g b", g=2, b=3)[:, :, :, 0]
            last = dve.tensor_tensor(fac, fac, gate, ALU.mult)
        own_dve(last)
        dve.tensor_tensor(cmp_p[:, :, :], cmp_p[:, :, :], bc(cmp_sum, 16, axis=2), ALU.mult).then_inc(S("cmp_p_ready"), 1)
        causal = const("causal", TT, T)
        for i in range(16 + 1):
            if i < 16:
                qt, nk = i // 8, (i // 8 + 1) * P
                dve.wait_ge(S("at_scores"), base + i + 1)
                if i >= 2:
                    dve.wait_ge(S("at_exp"), base + i - 1)
                for b in range(2):
                    last = dve.tensor_tensor_reduce(at_s[:, i % 2, b, 0:nk], bank(i % 2, 2, T)[:, b, 0:nk], causal[:, qt, 0:nk],
                                                    1.0, -3e38, ALU.add, ALU.max, at_max[:, i, b:b + 1])
                own_dve(last)
                dve.tensor_scalar(at_neg[:, i, :], at_max[:, i, :], -SCALE, None, ALU.mult).then_inc(S("at_arg"), 1)
            if i >= 1:
                j = i - 1
                qt, r, g = at_step(j)
                nk = (qt + 1) * P
                dve.wait_ge(S("at_exp"), base + j + 1)
                own_dve(dve.reciprocal(at_fac[:, j, :], at_sum[:, j, :]))
                own_dve(dve.tensor_tensor(at_fac[:, j, :], at_fac[:, j, :], gates[:, qt, 12 * g + 3 * r + 1:12 * g + 3 * r + 3], ALU.mult))
                p = at_p[:, j % 2, :, 0:nk]
                dve.tensor_tensor(p, p, bc(at_fac[:, j, :], nk, axis=2), ALU.mult).then_inc(S("at_p"), 1)
        dve.wait_ge(S("head_std"), 3 * l + 3)
        own_dve(dve.reciprocal(rn[:, 2:4, :], rn[:, 2:4, :]))
        own_dve(dve.tensor_tensor(h[:, 4:8], h[:, 4:8], rn[:, 2:4, :].rearrange("p a (b t) -> p (a b) t", t=T), ALU.mult))
        dve.tensor_scalar(h[:, 4:8], h[:, 4:8], param("nsa_norm_g", l, 1), None, ALU.mult).then_inc(S("y_ready"), 1)

    def back_pe(pe, first, call, source):
        for j in range(KT):
            pe.wait_ge(S("back_added"), (KT - 1) * call + max(j - 3, 0))
            wait_chunk(pe, first + j)
            for k in range(KT):
                mm = pe.matmul(bank(j % 4, T), chunk(first + j)[:, k], source[:, k], start=(k == 0), stop=(k == KT - 1))
            mm.then_inc(S("chunk_used"), 1)

    def back_dve(dve, first, call, gate_col=None):
        for j in range(KT):
            dve.wait_ge(S("chunk_used"), first + j + 1)
            if gate_col is None:
                ins = dve.tensor_tensor(xt[:, j], bank(j % 4, T), xt[:, j], ALU.add)
            else:
                ins = dve.scalar_tensor_tensor(xt[:, j], bank(j % 4, T), gate_col[:, j:j + 1], xt[:, j], ALU.mult, ALU.add)
            ins.then_inc(S("back_added"), 1) if j < KT - 1 else ins.then_inc(S("x_ready"), 1)

    lat = place(0, 6, T)
    lat_rn = place(1536, 2, T)
    q_mla, k_mla, v_mla = place(2048, 8, T), place(4096, 8, T), place(6144, TT, 512)
    o_mla = place(7744, 4, T)
    ml_p, ml_pt = place(9252, 2, 2, T), place(10276, 2, 4, P)
    ml_max, ml_neg, ml_sum, ml_fac = (place(11300 + 16 * n, 8, 2) for n in range(4))
    ML_SCALE = 96.0 ** -0.5
    ML_BASE = 16 * DEPTH

    def mla_pe(pe):
        first = STREAM["mla"]
        pe.wait_ge(S("h_ready"), 7)
        for j in range(6):
            pe.wait_ge(S("mla_evac"), max(j - 3, 0))
            wait_chunk(pe, first + j)
            for k in range(KT):
                mm = pe.matmul(bank(4 + j % 4, T), chunk(first + j)[:, k], h[:, k], start=(k == 0), stop=(k == KT - 1))
            mm.then_inc(S("chunk_used"), 1)
        pe.wait_ge(S("head_squared"), 3 * DEPTH + 1)
        for n, (mean, tiles) in enumerate((("mean_q", range(0, 3)), ("mean_kv", range(3, 5)))):
            for k in tiles:
                mm = pe.matmul(bank(n, T), const(mean), sq[:, k], start=(k == tiles[0]), stop=(k == tiles[-1]))
        mm = pe.matmul(bank(3, T), const("perm_mla"), lat[:, 5], start=True, stop=True)
        mm.then_inc(S("head_ms"), 1)
        pe.wait_ge(S("lat_normed"), 1)
        ended = False
        for name, at, parts, evac in (("uq", 0, 3, 6), ("ukv", 3, 2, 14)):
            for hd in range(8):
                n = evac + hd
                pe.wait_ge(S("mla_evac"), min(n - 3, 14))
                if n >= 18:
                    pe.wait_ge(S("k_evac"), n - 17)
                for k in range(parts):
                    block = hd * parts + k
                    i = STREAM[name] + block // 8
                    if block % 8 == 0:
                        wait_chunk(pe, i)
                    mm = pe.matmul(bank(4 + n % 4, T), chunk(i)[:, block % 8], lat[:, at + k], start=(k == 0), stop=(k == parts - 1))
                    if k < parts - 1 and (block % 8 == 7 or ended):
                        mm.then_inc(S("chunk_used"), 1)
                        ended = False
                mm.then_inc(S("head_tile"), 1)
                ended = block % 8 == 7
        i = STREAM["ukv"] + 2
        wait_chunk(pe, i)
        for t in range(TT):
            for k in range(2):
                w = chunk(i).rearrange("p a b -> p (a b)")[:, k * 512:(k + 1) * 512]
                mm = pe.matmul(bank(2 + t), lat[:, 3 + k, t * P:(t + 1) * P], w, start=(k == 0), stop=(k == 1))
                if t == 0 and k == 0:
                    mm.then_inc(S("chunk_used"), 1)
        mm.then_inc(S("chunk_used"), 1)
        pe.wait_ge(S("mla_evac"), 14)
        pe.wait_ge(S("k_evac"), 8)
        for b in range(4):
            mm = pe.matmul(bank(4 + b), const("perm_mla"), q_mla[:, 2 * b:2 * b + 2, :], start=True, stop=True)
        mm.then_inc(S("q_rotated"), 1)
        pe.wait_ge(S("q_roped"), 1)
        for i in range(8 + 2):
            if i < 8:
                qt, pair = i // 4, i % 4
                if i >= 2:
                    pe.wait_ge(S("at_exp"), ML_BASE + i - 1)
                else:
                    pe.wait_ge(S("v_mla_ready"), 1)
                for e in range(2):
                    hd = 2 * pair + e
                    mm = pe.matmul(bank(2 * (i % 2) + e, T), q_mla[:, hd, qt * P:(qt + 1) * P], k_mla[:, hd], start=True, stop=True)
                mm.then_inc(S("at_scores"), 1)
            if 1 <= i <= 8:
                j = i - 1
                pe.wait_ge(S("at_p"), ML_BASE + j + 1)
                if j >= 2:
                    pe.wait_ge(S("at_pt"), ML_BASE + j - 1)
                for e in range(2):
                    for t in range(TT):
                        mm = pe.transpose(bank(4 + j % 2, 4, P)[:, 2 * e + t], ml_p[:, j % 2, e, t * P:(t + 1) * P], ident)
                mm.then_inc(S("at_turned"), 1)
            if i >= 2:
                j = i - 2
                pair = j % 4
                pe.wait_ge(S("at_pt"), ML_BASE + j + 1)
                if j >= 2:
                    pe.wait_ge(S("at_y"), ML_BASE + j - 1)
                for e in range(2):
                    for t in range(TT):
                        mm = pe.matmul(bank(6 + j % 2, 2, P)[:, e], v_mla[:, t, pair * P:(pair + 1) * P], ml_pt[:, j % 2, 2 * e + t],
                                       start=(t == 0), stop=(t == TT - 1))
                mm.then_inc(S("at_o"), 1)

    def mla_act(act):
        first = STREAM["mla"]
        for j in range(6):
            act.wait_ge(S("chunk_used"), first + j + 1)
            act.activation(lat[:, j], bank(4 + j % 4, T), ACT.Copy).then_inc(S("mla_evac"), 1)
        act.wait_ge(S("mla_evac"), 6)
        act.activation(sq[:, 0:5, :], lat[:, 0:5], ACT.Square).then_inc(S("head_squared"), 1)
        act.wait_ge(S("head_ms"), 3 * DEPTH + 1)
        for n in range(2):
            last = act.activation(lat_rn[:, n], bank(n, T), ACT.Sqrt, bias=eps_c)
        last.then_inc(S("head_std"), 1)
        for hd in range(8):
            act.wait_ge(S("head_tile"), hd + 1)
            act.activation(q_mla[:, hd], bank(4 + (6 + hd) % 4, T), ACT.Copy).then_inc(S("mla_evac"), 1)
        act.wait_ge(S("chunk_used"), STREAM["ukv"] + 3)
        act.activation(v_mla[:, :, :], ps[:, 2:4, :], ACT.Copy).then_inc(S("v_mla_ready"), 1)
        for i in range(8 + 2):
            if i < 8:
                act.wait_ge(S("at_arg"), ML_BASE + i + 1)
                if i >= 2:
                    act.wait_ge(S("at_turned"), ML_BASE + i - 1)
                for e in range(2):
                    last = act.activation(ml_p[:, i % 2, e], bank(2 * (i % 2) + e, T), ACT.Exp, bias=ml_neg[:, i, e:e + 1],
                                          scale=ML_SCALE, accum_out=ml_sum[:, i, e:e + 1])
                last.then_inc(S("at_exp"), 1)
            if 1 <= i <= 8:
                j = i - 1
                act.wait_ge(S("at_turned"), ML_BASE + j + 1)
                if j >= 2:
                    act.wait_ge(S("at_o"), ML_BASE + j - 1)
                act.activation(ml_pt[:, j % 2], bank(4 + j % 2, 4, P), ACT.Copy).then_inc(S("at_pt"), 1)
            if i >= 2:
                j = i - 2
                act.wait_ge(S("at_o"), ML_BASE + j + 1)
                for e in range(2):
                    half = slice(64 * e, 64 * e + 64)
                    last = act.activation(o_mla[half, j % 4, j // 4 * P:(j // 4 + 1) * P], ps[half, 6 + j % 2, e * P:(e + 1) * P], ACT.Copy)
                last.then_inc(S("at_y"), 1)

    def mla_dve(dve):
        own_dve = own(dve, "dve_step")
        dve.wait_ge(S("head_std"), 3 * DEPTH + 1)
        cos, sin = const("cos_mla"), const("sin_mla")
        dve.tensor_tensor(sq[:, 6], bank(3, T), sin, ALU.mult)
        own_dve(dve.tensor_tensor(lat[:, 5], lat[:, 5], cos, ALU.mult))
        own_dve(dve.tensor_tensor(lat[:, 5], lat[:, 5], sq[:, 6], ALU.add))
        own_dve(dve.reciprocal(lat_rn[:, :, :], lat_rn[:, :, :]))
        for n, tiles in enumerate((slice(0, 3), slice(3, 5))):
            last = dve.tensor_tensor(lat[:, tiles], lat[:, tiles], bc(lat_rn[:, n], tiles.stop - tiles.start), ALU.mult)
        own_dve(last)
        for k in range(5):
            gain = param("q_norm_g", k, 1) if k < 3 else param("kv_norm_g", k - 3, 1)
            last = dve.tensor_scalar(lat[:, k], lat[:, k], gain, None, ALU.mult)
        last.then_inc(S("lat_normed"), 1)
        for hd in range(8):
            dve.wait_ge(S("head_tile"), 8 + hd + 1)
            dve.tensor_tensor(k_mla[:, hd], bank(4 + (14 + hd) % 4, T), lat[:, 5], ALU.add).then_inc(S("k_evac"), 1)
        dve.wait_ge(S("k_evac"), 8)
        dve.wait_ge(S("q_rotated"), 1)
        dve.tensor_tensor(sq[:, :, :], ps[:, 4:8, :].rearrange("p a (b t) -> p (a b) t", t=T), bc(sin, 8), ALU.mult)
        own_dve(dve.tensor_tensor(q_mla[:, :, :], q_mla[:, :, :], bc(cos, 8), ALU.mult))
        dve.tensor_tensor(q_mla[:, :, :], q_mla[:, :, :], sq[:, :, :], ALU.add).then_inc(S("q_roped"), 1)
        for i in range(8 + 1):
            if i < 8:
                dve.wait_ge(S("at_scores"), ML_BASE + i + 1)
                b = 2 * (i % 2)
                own_dve(dve.tensor_reduce(ml_max[:, i, :], ps[:, b:b + 2, 0:T], AX_X, ALU.max))
                dve.tensor_scalar(ml_neg[:, i, :], ml_max[:, i, :], -ML_SCALE, None, ALU.mult).then_inc(S("at_arg"), 1)
            if i >= 1:
                j = i - 1
                dve.wait_ge(S("at_exp"), ML_BASE + j + 1)
                own_dve(dve.reciprocal(ml_fac[:, j, :], ml_sum[:, j, :]))
                dve.tensor_tensor(ml_p[:, j % 2], ml_p[:, j % 2], bc(ml_fac[:, j, :], T, axis=2), ALU.mult).then_inc(S("at_p"), 1)

    zp, zf = place(8768, 15, T + 2), place(12638, 15, T)
    kk = place(11300, 4, T)
    rows_op = place(3072, 4, TT, 2, P)
    b_hat, k_hat2 = place(5120, 4, T), place(6144, 4, T)
    w_tok, u_neg = place(7168, 512), hid_raw[:, :, :].rearrange("p a t -> p (a t)")
    sig, aa, exp_r = place(16478, 4, T), place(17502, 4, T), place(18526, 4, T)
    mats = place(16478, 8, 3, P)
    dd, ee = place(19550, 4, T), place(20574, 4, T)
    exp_k, exp_inv, k_dir = place(0, 4, T), place(1024, 4, T), place(2048, 4, T)
    bonus, yw = place(21600, 4, T), place(22624, 4, T)
    s_zero = hidden[:, :, :].rearrange("p a (b t) -> p (a b) t", t=P)
    s_arg, s_dec = place(23648, 4), place(23652, 4)
    c_mid, one_less_ka = place(23656, 15), place(23672, 4)
    half_tot = place(23676, 4, TT)
    v_tok2 = sq[:, 0:4, :].rearrange("p (c a) t -> p c (a t)", c=TT)
    b_tok, k_tok2 = sq[:, 4:6, :].rearrange("p a t -> p (a t)"), sq[:, 6:8, :].rearrange("p a t -> p (a t)")

    def early_gates(d):
        return range(0, 3) if d == 0 else range(3, GATES_EARLY)

    def gate_tile(j):
        if j < 2:
            return silu_gate[:, j]
        if j == 2:
            return place(8768, T)
        if j < GATES_EARLY:
            return dd[:, j - 3]
        return gates_late[:, j - GATES_EARLY]

    def wkv_call(d, s):
        return DEPTH + 2 * d + s

    def wkv_chunk(d, s):
        return s if d == 0 else 1 - s

    def by_chunk(v):
        return v.rearrange("p a (c t) -> p a c t", t=P)

    def rwkv_pe(pe):
        first = STREAM["rwkv"]
        pe.wait_ge(S("at_y"), ML_BASE + 8)
        for j in range(15):
            pe.wait_ge(S("rw_evac"), max(j - 3, 0))
            wait_chunk(pe, first + j)
            for k in range(KT):
                mm = pe.matmul(bank(4 + j % 4, T), chunk(first + j)[:, k], h[:, k], start=(k == 0), stop=(k == KT - 1))
            mm.then_inc(S("chunk_used"), 1)
        pe.wait_ge(S("head_squared"), 3 * DEPTH + 2)
        for b in range(2):
            mm = pe.matmul(bank(b), block_ones, sq[:, 2 * b:2 * b + 2, :], start=True, stop=True)
        mm.then_inc(S("head_ms"), 1)
        pe.wait_ge(S("shifted"), 3)
        for c in range(TT):
            for ct in range(4):
                mm = pe.transpose(bank(2 + c, 4, P)[:, ct], zf[:, 8 + ct, c * P:(c + 1) * P], ident)
        mm.then_inc(S("rw_v_turned"), 1)
        pe.wait_ge(S("rw_v_ready"), 1)
        pe.wait_ge(S("head_std"), 3 * DEPTH + 2)
        pe.wait_ge(S("lora_in"), 1)
        up = STREAM["up"]
        wait_chunk(pe, up)
        for d in range(2):
            half = slice(64 * d, 64 * d + 64)
            if d == 1:
                pe.wait_ge(S("y_sum"), 2)
            for n in range(2):
                for ct in range(4):
                    mm = pe.matmul(bank(2 * n + ct // 2, 2, T)[:, ct % 2], chunk(up)[half, 4 * n + ct], zf[half, 12 + n],
                                   start=True, stop=True)
            mm.then_inc(S("lora_done"), 1)
            for n, j in enumerate(early_gates(d)):
                wait_chunk(pe, STREAM["gate"] + j)
                for k in range(KT):
                    mm = pe.matmul(bank(4 + n // 2, 2, T)[:, n % 2], chunk(STREAM["gate"] + j)[:, k], h[:, k],
                                   start=(k == 0), stop=(k == KT - 1))
                mm.then_inc(S("chunk_used"), 1)
            pe.wait_ge(S("wkv_operands"), d + 1)
            c = wkv_chunk(d, 0)
            for n, op in enumerate((b_hat, k_hat2)):
                for ct in range(4):
                    mm = pe.transpose(bank(6 + n, 4, P)[:, ct], op[:, ct, c * P:(c + 1) * P], ident)
            mm.then_inc(S("op_turned"), 1)
            pe.wait_ge(S("op_tok"), d + 1)
            for s in range(2):
                step, call, c = 2 * d + s, wkv_call(d, s), wkv_chunk(d, s)
                if s == 1:
                    pe.wait_ge(S("y_sum"), 2 * d + 1)
                    pe.wait_ge(S("s_ready"), d + 1)
                for hd in range(8):
                    ct, e = hd // 2, hd % 2
                    rows = slice(64 * e, 64 * e + 64)
                    for n, op in enumerate((b_hat, k_hat2)):
                        mm = pe.matmul(bank(hd, 2, T)[:, n], op[rows, ct, c * P:(c + 1) * P], rows_op[rows, ct, c, :, :],
                                       start=True, stop=True)
                mm.then_inc(S("wkv_products"), 1)
                pe.wait_ge(S("lt_ready"), 2 * call + 2)
                for ct in range(4):
                    if s == 1:
                        pe.matmul(bank(6, 4, P)[:, ct], rows_op[:, ct, c, 0, :], s_zero[:, ct], start=True, stop=False, skip_group_check=True)
                    for e in range(2):
                        hd = 2 * ct + e
                        mm = pe.matmul(bank(6, 8, 64)[:, hd], mats[:, hd, 1], v_tok2[:, c, hd * 64:hd * 64 + 64],
                                       start=(s == 0), stop=True, skip_group_check=True)
                mm.then_inc(S("w_done"), 1)
                inv_pe(pe, call)
                pe.wait_ge(S("w_ready"), step + 1)
                pe.wait_ge(S("x_updated"), 2 * INV_LEVELS * (call + 1))
                for hd in range(8):
                    mm = pe.matmul(bank(6, 8, 64)[:, hd], inv_xt[:, hd // 4, hd % 4], w_tok[:, hd * 64:hd * 64 + 64], start=True, stop=True)
                mm.then_inc(S("u_done"), 1)
                pe.wait_ge(S("u_ready"), step + 1)
                if s == 0:
                    for ct in range(4):
                        cols = slice(ct * P, (ct + 1) * P)
                        pe.matmul(bank(7, 4, P)[:, ct], b_tok[:, cols], u_neg[:, cols], start=True, stop=False)
                        mm = pe.matmul(bank(7, 4, P)[:, ct], k_tok2[:, cols], v_tok2[:, c, cols], start=False, stop=True)
                    mm.then_inc(S("s_done"), 1)
                for hd in range(8):
                    ct = hd // 2
                    cols = slice(ct * P, (ct + 1) * P)
                    o = bank(hd // 4, 4, P)[:, hd % 4]
                    pe.matmul(o, u_neg[:, cols], mats[:, hd, 0], start=True, stop=False)
                    mm = pe.matmul(o, v_tok2[:, c, cols], mats[:, hd, 2], start=False, stop=(s == 0))
                    if s == 1:
                        mm = pe.matmul(o, s_zero[:, ct], rows_op[:, ct, c, 1, :], start=False, stop=True)
                mm.then_inc(S("y_done"), 1)
        pe.wait_ge(S("y_sum"), 4)
        for b in range(2):
            mm = pe.matmul(bank(b), const("block_mean"), yw[:, 2 * b:2 * b + 2, :], start=True, stop=True)
        mm.then_inc(S("y_mean"), 1)
        for b in range(2):
            mm = pe.matmul(bank(4 + b), block_ones, bonus[:, 2 * b:2 * b + 2, :], start=True, stop=True)
        wait_chunk(pe, up + 1)
        mm.then_inc(S("chunk_used"), 1)
        for ct in range(4):
            mm = pe.matmul(bank(6 + ct // 2, 2, T)[:, ct % 2], chunk(up + 1)[:, ct], zf[:, 14], start=True, stop=True)
        mm.then_inc(S("chunk_used"), 1)
        pe.wait_ge(S("head_squared"), 3 * DEPTH + 3)
        for b in range(2):
            mm = pe.matmul(bank(2 + b), const("block_mean"), sq[:, 2 * b:2 * b + 2, :], start=True, stop=True)
        mm.then_inc(S("head_ms"), 1)

    def rwkv_act(act):
        first = STREAM["rwkv"]
        act.wait_ge(S("zp_zeroed"), 1)
        for j in range(15):
            act.wait_ge(S("chunk_used"), first + j + 1)
            act.activation(zp[:, j, 1:T + 1], bank(4 + j % 4, T), ACT.Copy).then_inc(S("rw_evac"), 1)
        act.wait_ge(S("kk_raw"), 1)
        act.activation(sq[:, 0:4, :], kk[:, :, :], ACT.Square).then_inc(S("head_squared"), 1)
        act.wait_ge(S("head_ms"), 3 * DEPTH + 2)
        act.activation(exp_r[:, :, :], ps[:, 0:2, :].rearrange("p a (b t) -> p (a b) t", t=T), ACT.Sqrt).then_inc(S("head_std"), 1)
        act.wait_ge(S("rw_v_turned"), 1)
        act.activation(v_tok2[:, :, :], ps[:, 2:4, :], ACT.Copy).then_inc(S("rw_v_ready"), 1)
        act.wait_ge(S("shifted"), 3)
        act.activation(zf[:, 12], zf[:, 12], ACT.Tanh)
        act.activation(zf[:, 14], zf[:, 14], ACT.Sigmoid).then_inc(S("lora_in"), 1)
        for d in range(2):
            act.wait_ge(S("lora_done"), d + 1)
            if d == 0:
                act.wait_ge(S("kk_unit"), 1)
            for n, (into, bias) in enumerate(((sig, "w0"), (aa, "a0"))):
                for ct in range(4):
                    last = act.activation(into[:, ct], bank(2 * n + ct // 2, 2, T)[:, ct % 2], ACT.Sigmoid, bias=param(bias, 4 * d + ct, 1))
            last.then_inc(S("sig_ready"), 1)
            act.wait_ge(S("expo_ready"), d + 1)
            for into, src, sign in ((exp_r, dd, -1), (exp_k, ee, -1), (exp_inv, dd, 1)) if d == 0 else \
                                   ((exp_r, ee, 1), (exp_k, dd, 1), (exp_inv, ee, -1)):
                act.activation(into[:, :, :], src[:, :, :], ACT.Exp, scale=sign * KAPPA)
            act.activation(s_dec, s_arg, ACT.Exp, scale=-KAPPA).then_inc(S("exps_ready"), 1)
            act.wait_ge(S("exps_ready"), d + 1)
            act.wait_ge(S("chunk_used"), STREAM["gate"] + early_gates(d)[-1] + 1)
            for n, j in enumerate(early_gates(d)):
                act.activation(gate_tile(j), bank(4 + n // 2, 2, T)[:, n % 2], ACT.Sigmoid, bias=param("gate_b", j, 1))
            act.wait_ge(S("op_turned"), d + 1)
            act.activation(b_tok, bank(6), ACT.Copy)
            act.activation(k_tok2, bank(7), ACT.Copy).then_inc(S("op_tok"), 1)
            for s in range(2):
                step, call, c = 2 * d + s, wkv_call(d, s), wkv_chunk(d, s)
                act.wait_ge(S("w_done"), step + 1)
                act.activation(w_tok, bank(6), ACT.Copy).then_inc(S("w_ready"), 1)
                inv_act(act, call)
                act.wait_ge(S("u_done"), step + 1)
                act.activation(u_neg, bank(6), ACT.Copy, scale=-1.0).then_inc(S("u_ready"), 1)
                if d == 0:
                    act.wait_ge(S("y_done"), step + 1)
                    for e in range(2):
                        rows = slice(64 * e, 64 * e + 64)
                        src = ps[rows, 0:2, :].rearrange("p b (c e t) -> p b c e t", e=2, t=P)[:, :, :, e, :]
                        dst = yw[rows, :, c * P:(c + 1) * P].rearrange("p (b c) t -> p b c t", b=2)
                        last = act.activation(dst, src, ACT.Copy)
                    last.then_inc(S("y_sum"), 1)
        act.wait_ge(S("y_centred"), 1)
        act.activation(sq[:, 0:4, :], yw[:, :, :], ACT.Square).then_inc(S("head_squared"), 1)
        act.wait_ge(S("head_ms"), 3 * DEPTH + 3)
        act.activation(exp_r[:, :, :], ps[:, 2:4, :].rearrange("p a (b t) -> p (a b) t", t=T), ACT.Sqrt, bias=const("lnx_eps")).then_inc(S("head_std"), 1)

    def rwkv_dve(dve):
        own_dve = own(dve, "dve_step")
        dve.wait_ge(S("at_y"), ML_BASE + 8)
        dve.memset(zp[:, :, 0:1], 0.0)
        dve.memset(zp[:, :, T + 1:T + 2], 0.0).then_inc(S("zp_zeroed"), 1)
        own_dve(dve.tensor_tensor(c_mid, param("mu_prev"), param("mu_next"), ALU.add))
        dve.tensor_scalar(one_less_ka, param("k_a"), -1.0, 1.0, ALU.mult, ALU.add)
        own_dve(dve.tensor_scalar(c_mid, c_mid, -1.0, 1.0, ALU.mult, ALU.add))
        for n in range(3):
            tiles = range(5 * n, 5 * n + 5)
            dve.wait_ge(S("rw_evac"), 5 * n + 5)
            for j in tiles:
                last = dve.tensor_scalar(zf[:, j], zp[:, j, 1:T + 1], c_mid[:, j:j + 1], None, ALU.mult)
            own_dve(last)
            for j in tiles:
                last = dve.scalar_tensor_tensor(zf[:, j], zp[:, j, 0:T], param("mu_prev", j, 1), zf[:, j], ALU.mult, ALU.add)
            own_dve(last)
            for j in tiles:
                last = dve.scalar_tensor_tensor(zf[:, j], zp[:, j, 2:T + 2], param("mu_next", j, 1), zf[:, j], ALU.mult, ALU.add)
            last.then_inc(S("shifted"), 1)
        dve.wait_ge(S("shifted"), 3)
        r, k, v = zf[:, 0:4], zf[:, 4:8], zf[:, 8:12]
        for ct in range(4):
            last = dve.tensor_scalar(kk[:, ct], k[:, ct], param("k_k", ct, 1), None, ALU.mult)
        last.then_inc(S("kk_raw"), 1)
        dve.wait_ge(S("head_std"), 3 * DEPTH + 2)
        own_dve(dve.tensor_scalar(exp_r[:, :, :], exp_r[:, :, :], 1e-12, None, ALU.max))
        own_dve(dve.reciprocal(exp_r[:, :, :], exp_r[:, :, :]))
        own_dve(dve.memset(s_zero[:, :, :], 0.0))
        dve.tensor_tensor(kk[:, :, :], kk[:, :, :], exp_r[:, :, :], ALU.mult).then_inc(S("kk_unit"), 1)
        dve.wait_ge(S("kk_unit"), 1)
        for d in range(2):
            dve.wait_ge(S("sig_ready"), d + 1)
            dd4 = by_chunk(dd)
            for ct in range(4):
                for c in range(TT):
                    last = dve.tensor_tensor_scan(dd4[:, ct, c], ones, sig[:, ct, c * P:(c + 1) * P], 0.0, ALU.mult, ALU.add)
            own_dve(last)
            own_dve(dve.tensor_scalar(half_tot[:, :, :], dd4[:, :, :, P - 1], 0.5, None, ALU.mult))
            dve.tensor_tensor(s_arg, half_tot[:, :, 0], half_tot[:, :, 1], ALU.add)
            own_dve(dve.tensor_tensor(dd4, dd4, half_tot[:, :, :].unsqueeze(3).broadcast_to((P, 4, TT, P)), ALU.subtract))
            dve.tensor_tensor(ee[:, :, :], dd[:, :, :], sig[:, :, :], ALU.subtract).then_inc(S("expo_ready"), 1)
            for ct in range(4):
                last = dve.tensor_scalar(k_dir[:, ct], aa[:, ct], param("k_a", ct, 1), one_less_ka[:, ct:ct + 1], ALU.mult, ALU.add)
            own_dve(last)
            own_dve(dve.tensor_tensor(k_dir[:, :, :], k_dir[:, :, :], k, ALU.mult))
            dve.tensor_tensor(aa[:, :, :], aa[:, :, :], kk[:, :, :], ALU.mult)
            into = bonus if d == 0 else b_hat
            for ct in range(4):
                last = dve.scalar_tensor_tensor(into[:, ct], k_dir[:, ct], param("r_k", ct, 1), r[:, ct], ALU.mult, ALU.mult)
            own_dve(last)
            if d == 1:
                own_dve(dve.tensor_tensor(bonus[:, :, :], bonus[:, :, :], b_hat[:, :, :], ALU.add))
            dve.wait_ge(S("exps_ready"), d + 1)
            dve.tensor_tensor(rows_op[:, :, :, 0, :], by_chunk(kk), by_chunk(exp_k), ALU.mult)
            dve.tensor_tensor(rows_op[:, :, :, 1, :], by_chunk(r), by_chunk(exp_r), ALU.mult)
            dve.tensor_tensor(b_hat[:, :, :], aa[:, :, :], exp_inv[:, :, :], ALU.mult)
            dve.tensor_tensor(k_hat2[:, :, :], k_dir[:, :, :], exp_inv[:, :, :], ALU.mult).then_inc(S("wkv_operands"), 1)
            dve.wait_ge(S("wkv_operands"), d + 1)
            dve.memset(inv_lt[:, :, :, :], 0.0)
            own_dve(dve.memset(mats[:, :, :, :], 0.0))
            masks = const("wkv_masks", 2 * 3, P)[:, 3 * d:3 * d + 3, :].bitcast(I32)
            for s in range(2):
                step, call, c = 2 * d + s, wkv_call(d, s), wkv_chunk(d, s)
                dve.wait_ge(S("wkv_products"), step + 1)
                for hd in range(8):
                    dve.copy_predicated(mats[:, hd], masks, bank(hd, 4, P)[:, 1:4])
                    last = dve.copy_predicated(inv_lt[:, hd // 4, hd % 4], masks[:, 1], bank(hd, 4, P)[:, 0])
                    if hd % 4 == 3:
                        last.then_inc(S("lt_ready"), 1)
                inv_dve(dve, call)
                if s == 0:
                    dve.wait_ge(S("s_done"), d + 1)
                    for e in range(2):
                        rows = slice(64 * e, 64 * e + 64)
                        last = dve.tensor_tensor(s_zero[rows, :, 64 * e:64 * e + 64], bank(7, 4, P)[rows, :, 64 * e:64 * e + 64],
                                                 bc(s_dec[rows, :], 64, axis=2), ALU.mult)
                    last.then_inc(S("s_ready"), 1)
                if d == 1:
                    dve.wait_ge(S("y_done"), step + 1)
                    for e in range(2):
                        rows = slice(64 * e, 64 * e + 64)
                        src = ps[rows, 0:2, :].rearrange("p b (c e t) -> p b c e t", e=2, t=P)[:, :, :, e, :]
                        dst = yw[rows, :, c * P:(c + 1) * P].rearrange("p (b c) t -> p b c t", b=2)
                        last = dve.tensor_tensor(dst, dst, src, ALU.add)
                    last.then_inc(S("y_sum"), 1)
                else:
                    dve.wait_ge(S("y_sum"), step + 1)
        dve.wait_ge(S("y_mean"), 1)
        tiles = lambda b: ps[:, b:b + 2, :].rearrange("p a (b t) -> p (a b) t", t=T)
        dve.tensor_tensor(yw[:, :, :], yw[:, :, :], tiles(0), ALU.subtract).then_inc(S("y_centred"), 1)
        dve.wait_ge(S("head_std"), 3 * DEPTH + 3)
        own_dve(dve.reciprocal(exp_r[:, :, :], exp_r[:, :, :]))
        own_dve(dve.tensor_tensor(yw[:, :, :], yw[:, :, :], exp_r[:, :, :], ALU.mult))
        for ct in range(4):
            last = dve.tensor_scalar(yw[:, ct], yw[:, ct], param("lnx_g", ct, 1), param("lnx_b", ct, 1), ALU.mult, ALU.add)
        own_dve(last)
        dve.wait_ge(S("chunk_used"), STREAM["up"] + 2)
        own_dve(dve.tensor_tensor(bonus[:, :, :], tiles(4), v, ALU.mult))
        own_dve(dve.tensor_tensor(yw[:, :, :], yw[:, :, :], bonus[:, :, :], ALU.add))
        dve.tensor_tensor(yw[:, :, :], yw[:, :, :], tiles(6), ALU.mult).then_inc(S("rwkv_out"), 1)

    gates_late = place(0, 16 - GATES_EARLY, T)
    mixed_part = place(4096, 2, T)

    def merge_pe(pe):
        first = STREAM["gate_late"]
        pe.wait_ge(S("head_std"), 3 * DEPTH + 3)
        for j in range(16 - GATES_EARLY):
            pe.wait_ge(S("gate_evac"), max(j - 3, 0))
            wait_chunk(pe, first + j)
            for k in range(KT):
                mm = pe.matmul(bank(j % 4, T), chunk(first + j)[:, k], h[:, k], start=(k == 0), stop=(k == KT - 1))
            mm.then_inc(S("chunk_used"), 1)
        pe.wait_ge(S("rwkv_out"), 1)
        for n, (name, src) in enumerate((("br_mla", o_mla), ("br_rwkv", yw))):
            for j in range(KT):
                i = STREAM[name] + j // 2
                pe.wait_ge(S("branch_evac"), max(KT * n + j - 3, 0))
                if j % 2 == 0:
                    wait_chunk(pe, i)
                for k in range(4):
                    mm = pe.matmul(bank(4 + j % 4, T), chunk(i)[:, 4 * (j % 2) + k], src[:, k], start=(k == 0), stop=(k == 3))
                mm.then_inc(S("branch_tile" if j % 2 == 0 else "chunk_used"), 1)
        pe.wait_ge(S("branch_evac"), 2 * KT)
        back_pe(pe, STREAM["out"], DEPTH, sq)

    def merge_act(act):
        for j in range(16 - GATES_EARLY):
            act.wait_ge(S("chunk_used"), STREAM["gate_late"] + j + 1)
            act.activation(gate_tile(GATES_EARLY + j), bank(j % 4, T), ACT.Sigmoid, bias=param("gate_b", GATES_EARLY + j, 1))\
               .then_inc(S("gate_evac"), 1)

    def merge_dve(dve):
        own_dve = own(dve, "dve_step")
        dve.wait_ge(S("gate_evac"), 16 - GATES_EARLY)
        for n, name in enumerate(("br_mla", "br_rwkv")):
            for j in range(KT):
                if j % 2 == 0:
                    dve.wait_ge(S("branch_tile"), 4 * n + j // 2 + 1)
                else:
                    dve.wait_ge(S("chunk_used"), STREAM[name] + j // 2 + 1)
                if n == 0:
                    dve.tensor_tensor(sq[:, j], bank(4 + j % 4, T), gate_tile(j), ALU.mult).then_inc(S("branch_evac"), 1)
                else:
                    own_dve(dve.tensor_tensor(mixed_part[:, j % 2], bank(4 + j % 4, T), gate_tile(KT + j), ALU.mult))
                    dve.tensor_tensor(sq[:, j], sq[:, j], mixed_part[:, j % 2], ALU.add).then_inc(S("branch_evac"), 1)
        back_dve(dve, STREAM["out"], DEPTH)

    weight_rows = place(0, N_EXP, T)
    logit_t = place(8192, T)
    logits, shown = place(8448, TT, 36), place(8520, TT, 4)
    g_eq, g_at, g_hot, g_pen = (place(8528 + 8 * n, TT, 4) for n in range(4))
    e_masked, e_eq, e_at, e_hot1, e_hot2, e_weight = (place(8560 + 64 * n, TT, 32) for n in range(6))
    g_max, g_idx, g_sum, m1, m2, e_idx, e_gap, e_exp, e_w1, e_w2 = (place(8944 + 2 * n, TT) for n in range(10))
    weight_t = place(9000, T)

    def route_pe(pe):
        pe.wait_ge(S("h_ready"), 8)
        for k in range(KT):
            mm = pe.matmul(ps[0:36, 0, 0:T], param("router_w", 36 * k, 36), h[:, k], start=(k == 0), stop=(k == KT - 1))
        mm.then_inc(S("logits_done"), 1)
        pe.wait_ge(S("logits_t"), 1)
        for t in range(TT):
            mm = pe.transpose(bank(1, TT, 36)[:, t], logit_t[0:36, t * P:(t + 1) * P], ident[0:36, 0:36])
        mm.then_inc(S("logits_turned"), 1)
        pe.wait_ge(S("weights_ready"), 1)
        for t in range(TT):
            mm = pe.transpose(ps[0:N_EXP, 2, t * P:(t + 1) * P], e_weight[:, t, :], ident)
        mm.then_inc(S("weights_turned"), 1)
        pe.wait_ge(S("weights_t"), 1)
        for n in range(N_EXP // 2):
            if n >= 4:
                pe.wait_ge(S("weight_rows"), n - 3)
            for e in range(2):
                one_hot = ident[0:N_EXP, 2 * n + e:2 * n + e + 1].broadcast_to((N_EXP, P))
                mm = pe.matmul(bank(4 + n % 4, 2, T)[:, e], one_hot, weight_t[0:N_EXP, :], start=True, stop=True)
            mm.then_inc(S("weight_rows_done"), 1)
        pe.wait_ge(S("weight_rows"), N_EXP // 2)

    def route_act(act):
        act.wait_ge(S("logits_done"), 1)
        act.activation(logit_t[0:36, :], ps[0:36, 0, 0:T], ACT.Copy).then_inc(S("logits_t"), 1)
        act.wait_ge(S("group_arg"), 1)
        act.activation(shown[:, :, :], shown[:, :, :], ACT.Exp).then_inc(S("group_exp"), 1)
        act.wait_ge(S("gap_ready"), 1)
        act.activation(e_exp, e_gap, ACT.Exp).then_inc(S("gap_exp"), 1)
        act.wait_ge(S("weights_turned"), 1)
        act.activation(weight_t[0:N_EXP, :], ps[0:N_EXP, 2, 0:T], ACT.Copy).then_inc(S("weights_t"), 1)
        for n in range(N_EXP // 2):
            act.wait_ge(S("weight_rows_done"), n + 1)
            act.activation(weight_rows[:, 2 * n:2 * n + 2, :], bank(4 + n % 4, 2, T), ACT.Copy).then_inc(S("weight_rows"), 1)

    def route_dve(dve):
        own_dve = own(dve, "dve_step")
        iota = const("iota")

        def first_largest(values, n, top, eq, at, idx, hot):
            own_dve(dve.tensor_reduce(top, values, AX_X, ALU.max))
            own_dve(dve.tensor_tensor(eq, values, bc(top, n, axis=2), ALU.is_equal))
            own_dve(dve.scalar_tensor_tensor(at, eq, -1000.0, bc(iota[:, 0:n], TT), ALU.mult, ALU.add))
            own_dve(dve.tensor_reduce(idx, at, AX_X, ALU.min))
            own_dve(dve.tensor_tensor(hot, at, bc(idx, n, axis=2), ALU.is_equal))

        dve.wait_ge(S("logits_turned"), 1)
        own_dve(dve.tensor_tensor(logits[:, :, :], bank(1, TT, 36), bc(param("router_b"), TT), ALU.add))
        groups, experts = logits[:, :, 0:N_GRP], logits[:, :, N_GRP:36]
        first_largest(groups, N_GRP, g_max, g_eq[:, :, :], g_at[:, :, :], g_idx, g_hot[:, :, :])
        dve.tensor_tensor(shown[:, :, :], groups, bc(g_max, N_GRP, axis=2), ALU.subtract).then_inc(S("group_arg"), 1)
        own_dve(dve.tensor_scalar(g_pen[:, :, :], g_hot[:, :, :], 1.0, BIG, ALU.subtract, ALU.mult))
        per = N_EXP // N_GRP
        for t in range(TT):
            last = dve.tensor_tensor(e_masked[:, t].rearrange("p (g e) -> p g e", e=per), experts[:, t].rearrange("p (g e) -> p g e", e=per),
                                     bc(g_pen[:, t], per, axis=2), ALU.add)
        own_dve(last)
        first_largest(e_masked[:, :, :], N_EXP, m1, e_eq[:, :, :], e_at[:, :, :], e_idx, e_hot1[:, :, :])
        own_dve(dve.scalar_tensor_tensor(e_masked[:, :, :], e_hot1[:, :, :], -BIG, e_masked[:, :, :], ALU.mult, ALU.add))
        first_largest(e_masked[:, :, :], N_EXP, m2, e_eq[:, :, :], e_at[:, :, :], e_idx, e_hot2[:, :, :])
        dve.tensor_tensor(e_gap, m2, m1, ALU.subtract).then_inc(S("gap_ready"), 1)
        dve.wait_ge(S("group_exp"), 1)
        own_dve(dve.tensor_reduce(g_sum, shown[:, :, :], AX_X, ALU.add))
        dve.wait_ge(S("gap_exp"), 1)
        own_dve(dve.tensor_scalar(e_w1, e_exp, 1.0, None, ALU.add))
        own_dve(dve.tensor_tensor(e_w1, e_w1, g_sum, ALU.mult))
        own_dve(dve.reciprocal(e_w1, e_w1))
        own_dve(dve.tensor_tensor(e_w2, e_w1, e_exp, ALU.mult))
        dve.tensor_tensor(e_hot1[:, :, :], e_hot1[:, :, :], bc(e_w1, N_EXP, axis=2), ALU.mult)
        own_dve(dve.tensor_tensor(e_hot2[:, :, :], e_hot2[:, :, :], bc(e_w2, N_EXP, axis=2), ALU.mult))
        dve.tensor_tensor(e_weight[:, :, :], e_hot1[:, :, :], e_hot2[:, :, :], ALU.add).then_inc(S("weights_ready"), 1)

    with nc.Block() as block:
        @block.sync
        def _(sp):
            stream_sp(sp)
            sp.wait_ge(S("x_ready"), 3 * DEPTH + 4)
            sp.dma_start(out, xt[:, :, :]).then_inc(S("out_stored"), 16)
            sp.wait_ge(S("out_stored"), 16)

        @block.tensor
        def _(pe):
            ada_first_pe(pe)
            norm_pe(pe, 0)
            ada_columns_pe(pe, 0)
            for l in range(DEPTH):
                ffn_pe(pe, FT, STREAM["ffn0", l], 2 * l * FT, 3 * l + 1)
                ada_sums_pe(pe, 2 * l + 1, 0)
                norm_pe(pe, 3 * l + 1)
                ada_sums_pe(pe, 2 * l + 1, 1)
                ada_columns_pe(pe, 2 * l + 1)
                mix_pe(pe, l)
                gdn_pe(pe, l)
                nsa_pe(pe, l)
                pe.wait_ge(S("y_ready"), 2 * l + 2)
                back_pe(pe, STREAM["mixout", l], l, h)
                norm_pe(pe, 3 * l + 2)
                ffn_pe(pe, FT, STREAM["ffn1", l], (2 * l + 1) * FT, 3 * l + 3)
                if l + 1 < DEPTH:
                    ada_sums_pe(pe, 2 * l + 2, 0)
                    norm_pe(pe, 3 * l + 3)
                    ada_sums_pe(pe, 2 * l + 2, 1)
                    ada_columns_pe(pe, 2 * l + 2)
            norm_pe(pe, 6)
            norm_pe(pe, 7)
            mla_pe(pe)
            rwkv_pe(pe)
            merge_pe(pe)
            norm_pe(pe, 8)
            route_pe(pe)
            ffn_pe(pe, ET, STREAM["moe"], 4 * FT, 8)
            norm_pe(pe, 9)

        @block.scalar
        def _(act):
            setup_act(act)
            for l in range(DEPTH):
                norm_act(act, 3 * l)
                ffn_act(act, FT, STREAM["ffn0", l], 2 * l * FT)
                norm_act(act, 3 * l + 1)
                mix_act(act, l)
                gdn_act(act, l)
                nsa_act(act, l)
                norm_act(act, 3 * l + 2)
                ffn_act(act, FT, STREAM["ffn1", l], (2 * l + 1) * FT)
            norm_act(act, 6)
            norm_act(act, 7)
            mla_act(act)
            rwkv_act(act)
            merge_act(act)
            norm_act(act, 8)
            route_act(act)
            ffn_act(act, ET, STREAM["moe"], 4 * FT)
            norm_act(act, 9)

        @block.gpsimd
        def _(pool):
            for l in range(DEPTH):
                ada_pool(pool, 2 * l + 1)
                inv_pool(pool, l, 0, gdn_lt(l) + 2)
                if l + 1 < DEPTH:
                    ada_pool(pool, 2 * l + 2)
            for d in range(2):
                for s in range(2):
                    inv_pool(pool, wkv_call(d, s), d, 2 * wkv_call(d, s) + 2)

        @block.vector
        def _(dve):
            setup_dve(dve)
            for l in range(DEPTH):
                norm_dve(dve, 3 * l, mod_a[:, 0], mod[:, 0:KT], ada_call=2 * l)
                ffn_dve(dve, FT, STREAM["ffn0", l], 2 * l * FT, mod_g[:, 0], ada_call=2 * l + 1)
                norm_dve(dve, 3 * l + 1, mod_a[:, 1], mod[:, 3 * KT:4 * KT], ada_call=2 * l + 1)
                mix_dve(dve, l)
                gdn_dve(dve, l)
                nsa_dve(dve, l)
                back_dve(dve, STREAM["mixout", l], l, mod_g[:, 1])
                norm_dve(dve, 3 * l + 2, mod_a[:, 2], mod[:, 6 * KT:7 * KT])
                ffn_dve(dve, FT, STREAM["ffn1", l], (2 * l + 1) * FT, mod_g[:, 2], ada_call=2 * l + 2 if l + 1 < DEPTH else None)
            norm_dve(dve, 6, param("final_g"), into=xt)
            norm_dve(dve, 7, param("norm_mix_g"))
            mla_dve(dve)
            rwkv_dve(dve)
            merge_dve(dve)
            norm_dve(dve, 8, param("norm_ffn_g"))
            route_dve(dve)
            ffn_dve(dve, ET, STREAM["moe"], 4 * FT, None, weight_rows)
            norm_dve(dve, 9, param("norm_final_g"), into=xt)


def kernel(**inputs):
    import concourse.bacc as bacc
    from concourse.bass_utils import run_bass_kernel_spmd

    packed = pack({k: np.asarray(v) for k, v in inputs.items()})
    nc = bacc.Bacc("TRN2", target_bir_lowering=False, num_devices=1)
    names = ("weights", "params", "consts", "x_t", "pos")
    args = [nc.dram_tensor(f"in_{n}", packed[n].shape, mybir.dt.from_np(packed[n].dtype), kind="ExternalInput").ap()
            for n in names]
    args.append(nc.dram_tensor("out_t", (P, KT, T), F32, kind="ExternalOutput").ap())
    build(nc, *args)
    r = run_bass_kernel_spmd(nc, [{f"in_{n}": packed[n] for n in names}], core_ids=[0])
    return np.ascontiguousarray(r.results[0]["out_t"].transpose(2, 1, 0)).reshape(1, T, D)
```
